# Optimizing a Trainium2 kernel written in Bass

```python
import math
import jax, jax.numpy as jnp
from jax import lax
import numpy as np

D_MODEL = 2048
BATCH = 1
SEQ = 256
DEPTH = 1
DEC_BATCH = 8
DEC_SEQ = 1
PAST_LEN = 2048
PAGE_SIZE = 128

A_GROUPS = 8
A_GROUP_DIM = D_MODEL // 16
A_WIDTH = A_GROUPS * A_GROUP_DIM
CHUNK = 128
B_HEADS = 8
B_HEAD_K = 128
B_HEAD_V = D_MODEL // 16
B_KW = B_HEADS * B_HEAD_K
B_VW = B_HEADS * B_HEAD_V
HGRN_CHUNK = 64
N_EXPERTS = 16
N_EXPERT_GROUPS = 4
EXPERTS_PER_GROUP = N_EXPERTS // N_EXPERT_GROUPS
TOP_K = 2
D_FF = D_MODEL // 2
ALPHA = (2.0 * DEPTH) ** 0.25
BETA = (8.0 * DEPTH) ** -0.25
LN_EPS = 1e-5
IN_COLS = 2 * A_WIDTH + 2 * B_KW + 2 * B_VW + 2 * D_MODEL

kernel_name = "hybrid_sgu_hgrn2_grouped_moe_deepnorm_step"

def _split_points():
    sizes = [A_WIDTH, A_WIDTH, B_KW, B_KW, B_VW, B_VW, D_MODEL]
    return [int(s) for s in np.cumsum(sizes)]

def layer_norm(x, g, b):
    xf = x.astype(jnp.float32)
    mu = jnp.mean(xf, axis=-1, keepdims=True)
    var = jnp.mean(jnp.square(xf - mu), axis=-1, keepdims=True)
    y = (xf - mu) * lax.rsqrt(var + LN_EPS)
    return (y * g.astype(jnp.float32) + b.astype(jnp.float32)).astype(x.dtype)

def chunk_spatial_gating(u_pre, v_pre, ln_g, ln_b, w_s, b_s):
    B, T, _ = u_pre.shape
    L = min(T, CHUNK)
    u = jax.nn.gelu(u_pre)
    v = layer_norm(jax.nn.gelu(v_pre), ln_g, ln_b)
    causal = jnp.tril(jnp.ones((L, L), dtype=bool))
    w = jnp.where(causal[None], w_s[:, :L, :L], 0.0)
    vc = v.reshape(B, T // L, L, A_GROUPS, A_GROUP_DIM)
    s = jnp.einsum('gts,bnsgc->bntgc', w, vc) + b_s[:, :L].T[None, None, :, :, None]
    return u * s.reshape(B, T, A_WIDTH), v

def _hgrn2_chunk_step(S, inp):
    qc, kc, vc, gc = inp
    C = qc.shape[2]
    causal = jnp.tril(jnp.ones((C, C), dtype=bool))[None, None, :, :, None]
    diff = gc[:, :, :, None, :] - gc[:, :, None, :, :]
    decay = jnp.where(causal, jnp.exp(jnp.where(causal, diff, 0.0)), 0.0)
    scores = jnp.einsum('bhtd,bhsd,bhtsd->bhts', qc, kc, decay)
    o = (jnp.einsum('bhts,bhsv->bhtv', scores, vc)
         + jnp.einsum('bhtd,bhdv->bhtv', qc * jnp.exp(gc), S))
    g_last = gc[:, :, -1:, :]
    S_new = (jnp.exp(g_last[:, :, 0, :])[..., None] * S
             + jnp.einsum('bhsd,bhsv->bhdv', kc * jnp.exp(g_last - gc), vc))
    return S_new, o

def hgrn2_mix(q_pre, f_pre, i_pre, g_pre, lb, norm_g, S0):
    B, T, _ = q_pre.shape
    f32 = jnp.float32
    q = jax.nn.silu(q_pre.astype(f32)).reshape(B, T, B_HEADS, B_HEAD_K)
    z = f_pre.astype(f32).reshape(B, T, B_HEADS, B_HEAD_K)
    lb = lb.reshape(B_HEADS, B_HEAD_K)
    forget = lb + (1.0 - lb) * jax.nn.sigmoid(z)
    logf = jnp.log(forget)
    k = (1.0 - lb) * jax.nn.sigmoid(-z)
    v = i_pre.astype(f32).reshape(B, T, B_HEADS, B_HEAD_V)
    C = math.gcd(T, HGRN_CHUNK)
    N = T // C

    def to_chunks(a):
        return a.reshape(B, N, C, B_HEADS, a.shape[-1]).transpose(1, 0, 3, 2, 4)

    gcum = jnp.cumsum(to_chunks(logf), axis=3)
    S_final, o = lax.scan(_hgrn2_chunk_step, S0.astype(f32),
                          (to_chunks(q), to_chunks(k), to_chunks(v), gcum))
    o = o.transpose(1, 0, 3, 2, 4).reshape(B, T, B_HEADS, B_HEAD_V)
    o = o * lax.rsqrt(jnp.mean(jnp.square(o), axis=-1, keepdims=True) + LN_EPS)
    o = o.reshape(B, T, B_VW) * norm_g.astype(f32) * jax.nn.silu(g_pre.astype(f32))
    return o.astype(q_pre.dtype), S_final.astype(S0.dtype)

def moe_ffn(x, router_w, router_b, w_gate, w_up, w_down):
    B, T, D = x.shape
    f32 = jnp.float32
    xt = x.reshape(B * T, D)
    logits = (xt @ router_w).astype(f32) + router_b.astype(f32)
    probs = jax.nn.softmax(logits, axis=-1)
    grouped = probs.reshape(-1, N_EXPERT_GROUPS, EXPERTS_PER_GROUP)
    group_score = jnp.sum(lax.top_k(grouped, TOP_K)[0], axis=-1)
    sel_group = jnp.argmax(group_score, axis=-1)
    in_group = jnp.take_along_axis(grouped, sel_group[:, None, None], axis=1)[:, 0]
    top_w, top_i = lax.top_k(in_group, TOP_K)
    top_w = top_w / jnp.sum(top_w, axis=-1, keepdims=True)
    expert_ids = sel_group[:, None] * EXPERTS_PER_GROUP + top_i
    combine = jnp.sum(jax.nn.one_hot(expert_ids, N_EXPERTS, dtype=f32) * top_w[..., None], axis=1)
    y = jnp.zeros((B * T, D), f32)
    for e in range(N_EXPERTS):
        h = jax.nn.silu(xt @ w_gate[e]) * (xt @ w_up[e])
        y = y + combine[:, e:e + 1] * (h @ w_down[e]).astype(f32)
    return y.reshape(B, T, D).astype(x.dtype)

def decoder_layer(x, S0, lb, w_in, sgu_ln_g, sgu_ln_b, w_s, b_s, hgrn_norm_g, w_out_a, w_out_b,
                  w_o, ln1_g, ln1_b, router_w, router_b, w_gate, w_up, w_down, ln2_g, ln2_b):
    proj = jnp.einsum('btd,dc->btc', x, w_in)
    u_pre, v_pre, q_pre, f_pre, i_pre, g_pre, gate_a, gate_b = jnp.split(proj, _split_points(), axis=-1)
    y_a, v_rows = chunk_spatial_gating(u_pre, v_pre, sgu_ln_g, sgu_ln_b, w_s, b_s)
    y_b, S_new = hgrn2_mix(q_pre, f_pre, i_pre, g_pre, lb, hgrn_norm_g, S0)
    merged = jax.nn.sigmoid(gate_a) * (y_a @ w_out_a) + jax.nn.sigmoid(gate_b) * (y_b @ w_out_b)
    x = layer_norm(ALPHA * x + merged @ w_o, ln1_g, ln1_b)
    x = layer_norm(ALPHA * x + moe_ffn(x, router_w, router_b, w_gate, w_up, w_down), ln2_g, ln2_b)
    return x, S_new, v_rows

def trunk(x, init_states, lower_bounds, w_in, sgu_ln_g, sgu_ln_b, w_s, b_s, hgrn_norm_g, w_out_a,
          w_out_b, w_o, ln1_g, ln1_b, router_w, router_b, w_gate, w_up, w_down, ln2_g, ln2_b):
    states, v_rows = [], []
    for l in range(DEPTH):
        x, S, v = decoder_layer(x, init_states[l], lower_bounds[l], w_in[l], sgu_ln_g[l], sgu_ln_b[l],
                                w_s[l], b_s[l], hgrn_norm_g[l], w_out_a[l], w_out_b[l], w_o[l],
                                ln1_g[l], ln1_b[l], router_w, router_b, w_gate[l], w_up[l], w_down[l],
                                ln2_g[l], ln2_b[l])
        states.append(S)
        v_rows.append(v)
    return x, states, v_rows

def setup_inputs(seed: int = 0) -> dict:
    key = jax.random.key(seed)
    ks = jax.random.split(key, 24)
    f32 = jnp.float32

    def nrm(k, shape, scale):
        return scale * jax.random.normal(k, shape, f32)

    return {
        "x_prompt": nrm(ks[0], (BATCH, SEQ, D_MODEL), 1.0),
        "x_sample": nrm(ks[1], (DEC_BATCH, DEC_SEQ, D_MODEL), 1.0),
        "state_hgrn": nrm(ks[2], (DEPTH, DEC_BATCH, B_HEADS, B_HEAD_K, B_HEAD_V), 0.5),
        "w_in": nrm(ks[3], (DEPTH, D_MODEL, IN_COLS), D_MODEL ** -0.5),
        "sgu_ln_g": 1.0 + nrm(ks[4], (DEPTH, A_WIDTH), 0.02),
        "sgu_ln_b": nrm(ks[5], (DEPTH, A_WIDTH), 0.02),
        "w_s": nrm(ks[6], (DEPTH, A_GROUPS, CHUNK, CHUNK), CHUNK ** -0.5),
        "b_s": 1.0 + nrm(ks[7], (DEPTH, A_GROUPS, CHUNK), 0.1),
        "lb_logits": nrm(ks[8], (DEPTH, B_KW), 0.5),
        "hgrn_norm_g": 1.0 + nrm(ks[9], (DEPTH, B_VW), 0.02),
        "w_out_a": nrm(ks[10], (DEPTH, A_WIDTH, D_MODEL), BETA * A_WIDTH ** -0.5),
        "w_out_b": nrm(ks[11], (DEPTH, B_VW, D_MODEL), BETA * B_VW ** -0.5),
        "w_o": nrm(ks[12], (DEPTH, D_MODEL, D_MODEL), BETA * D_MODEL ** -0.5),
        "ln1_g": 1.0 + nrm(ks[13], (DEPTH, D_MODEL), 0.02),
        "ln1_b": nrm(ks[14], (DEPTH, D_MODEL), 0.02),
        "router_w": nrm(ks[15], (D_MODEL, N_EXPERTS), D_MODEL ** -0.5),
        "router_b": nrm(ks[16], (N_EXPERTS,), 0.01),
        "w_gate": nrm(ks[17], (DEPTH, N_EXPERTS, D_MODEL, D_FF), D_MODEL ** -0.5),
        "w_up": nrm(ks[18], (DEPTH, N_EXPERTS, D_MODEL, D_FF), D_MODEL ** -0.5),
        "w_down": nrm(ks[19], (DEPTH, N_EXPERTS, D_FF, D_MODEL), BETA * D_FF ** -0.5),
        "ln2_g": 1.0 + nrm(ks[20], (DEPTH, D_MODEL), 0.02),
        "ln2_b": nrm(ks[21], (DEPTH, D_MODEL), 0.02),
    }

def reference(x_prompt, x_sample, state_hgrn, w_in, sgu_ln_g, sgu_ln_b, w_s, b_s, lb_logits,
              hgrn_norm_g, w_out_a, w_out_b, w_o, ln1_g, ln1_b, router_w, router_b, w_gate, w_up,
              w_down, ln2_g, ln2_b):
    p = jax.nn.softmax(lb_logits.astype(jnp.float32), axis=0)
    lower_bounds = jnp.cumsum(p, axis=0) - p[0:1]

    zero_state = jnp.zeros((BATCH, B_HEADS, B_HEAD_K, B_HEAD_V), jnp.float32)
    y_prompt, s_prompt, _ = trunk(x_prompt, [zero_state] * DEPTH, lower_bounds, w_in, sgu_ln_g,
                                  sgu_ln_b, w_s, b_s, hgrn_norm_g, w_out_a, w_out_b, w_o, ln1_g,
                                  ln1_b, router_w, router_b, w_gate, w_up, w_down, ln2_g, ln2_b)
    y_sample, s_sample, v_sample = trunk(x_sample, [state_hgrn[l] for l in range(DEPTH)],
                                         lower_bounds, w_in, sgu_ln_g, sgu_ln_b, w_s, b_s,
                                         hgrn_norm_g, w_out_a, w_out_b, w_o, ln1_g, ln1_b,
                                         router_w, router_b, w_gate, w_up, w_down, ln2_g, ln2_b)
    state_hgrn_prompt = jnp.stack(s_prompt)
    state_hgrn_sample = jnp.stack(s_sample)
    state_chunk_v_sample = jnp.stack(v_sample)
    return (y_prompt, y_sample, state_hgrn_prompt, state_hgrn_sample, state_chunk_v_sample)


_drawn_inputs = setup_inputs


def setup_inputs(seed=0):
    import zlib

    import numpy as np

    out = dict(_drawn_inputs(seed))
    spreads = {}
    factors = {'sgu_ln_g': 22.142,
     'sgu_ln_b': 21.312,
     'hgrn_norm_g': 23.339,
     'ln2_g': 23.55,
     'ln2_b': 22.71,
     'router_b': 2.805,
     'b_s': 4.107}
    for name, (base, spread) in spreads.items():
        noise = np.random.default_rng([zlib.crc32(name.encode()), seed]).standard_normal(out[name].shape)
        drawn = base * np.exp(spread * noise) if base else spread * noise
        out[name] = __import__('jax').numpy.asarray(drawn.astype(out[name].dtype))
    for name, factor in factors.items():
        out[name] = (out[name] * factor).astype(out[name].dtype)
    return out
```

```python
from contextlib import ExitStack

import concourse.bass as bass
from concourse import mybir

F32 = mybir.dt.float32
I32 = mybir.dt.int32
ALU = mybir.AluOpType
ACT = mybir.ActivationFunctionType
AX = mybir.AxisListType

P = 128
D = 2048
NP_ = 256
NS = 8
T = NP_ + NS
KD = D // P
H = 8
W = H * P
FF = D // 2
E = 16
EG = 4
G4 = E // EG
CAP = 64
NOV = (2 * T) // CAP
NOVP = NOV // 2
NPAIR = E // 2
NITEM = E + NOV + 2
ALPHA = 2.0 ** 0.25
EPS = 1e-5
SLOT = 4096
FAR = 8192.0

GROUPS = [("f", 24, 8), ("q", 16, 8), ("i", 32, 8), ("v", 8, 8), ("u", 0, 8), ("g", 40, 8), ("ga", 48, 16), ("gb", 64, 16)]
N_IN = 80
N_OUT = 32
C_IN = N_IN // 2
C_ALL = C_IN + 8 + 8
UNITS = 24
LEVELS = 8


def start_of(name):
    n = 0
    for g, _, k in GROUPS:
        if g == name:
            return n
        n += k
    raise KeyError(name)


def build(nc, x_t, w_in, ws_t, w00, b_s, lng, lnb, lbl, normg, state, woa, wob, wo, ln1g, ln1b, rw, rb,
          wg, wu, wd, ln2g, ln2b, y, st_p, st_s, v_s):
    with ExitStack() as ctx:
        def sb(name, shape, dt=F32):
            return ctx.enter_context(nc.sbuf_tensor(name, shape, dt))

        def sem(name):
            return ctx.enter_context(nc.semaphore(name))

        scratch = nc.dram_tensor("expert_rows", [(E + NOV) * CAP, D], F32, kind="Internal").ap()

        ring = sb("ring", [P, 8, SLOT])
        xt = sb("xt", [P, KD, T])
        reg_uv = sb("reg_uv", [P, 3 * H * T])
        reg_pk = sb("reg_pk", [P, 2 * H * T])
        reg_qg = sb("reg_qg", [P, 2 * H * T])
        HT = H * T

        def fm(region, at, tiles):
            return region[:, at:at + tiles * T].rearrange("p (k t) -> p k t", t=T)

        vi = fm(reg_uv, 0, H)
        z = reg_uv[:, HT:HT + H * NP_].rearrange("p (k t) -> p k t", t=NP_)
        gb = fm(reg_uv, 0, 2 * H)
        u = fm(reg_uv, 2 * HT, H)
        pcum = fm(reg_pk, 0, H)
        kf = fm(reg_pk, HT, H)
        ga = fm(reg_pk, 0, 2 * H)
        qf = fm(reg_qg, 0, H)
        gf = fm(reg_qg, HT, H)

        up = ring[:, 4:8, :].rearrange("p a b -> p (a b)")
        scum = up[:, 0:2048].rearrange("p (k t) -> p k t", t=NP_)
        sc = up[:, 2048:4096].rearrange("p (h a t) -> p h a t", a=2, t=P)
        scx = up[:, 4096:5120].rearrange("p (h t) -> p h t", t=P)
        itm = up[:, 5120:8192].rearrange("p (a c) -> p a c", c=W)
        vtm = up[:, 8192:11264].rearrange("p (a c) -> p a c", c=W)
        wsm = up[:, 11264:12288].rearrange("p (g t) -> p g t", t=P)
        mask = up[:, 12288:13312].rearrange("p (l t) -> p l t", t=P)
        lngb = up[:, 13312:15360].rearrange("p (a c) -> p a c", c=W)
        bsb = up[:, 15360:16384].rearrange("p (g t) -> p g t", t=P)
        ktm = pcum.rearrange("p k t -> p (k t)")[:, 0:2048].rearrange("p (a c) -> p a c", c=W)
        s0b = [reg_uv[:, HT + 1024 * a:HT + 1024 * (a + 1)].rearrange("p (b v) -> p b v", v=P) for a in range(2)]
        vdb = [reg_uv[0:NS, 1024 * a:1024 * (a + 1)].rearrange("p (b v) -> p b v", v=P) for a in range(2)]

        x1 = reg_uv[:, 3 * HT - 3 * D:3 * HT].rearrange("p (a c) -> p a c", c=D)
        xg = reg_pk[:, 0:KD * P].rearrange("p (k s) -> p k s", s=P)
        lnp = reg_qg[:, 0:2 * D].rearrange("p (a c) -> p a c", c=D)
        xtf = xt[:, :, :].rearrange("p k t -> p (k t)")
        hid = [xtf[:, 512 * a:512 * (a + 1)] for a in range(2)]
        hidt = [xtf[:, 1024 + 512 * a:1536 + 512 * a].rearrange("p (j f s) -> p j f s", j=4, f=2) for a in range(2)]
        ob = [xtf[:, 2048 + 1024 * a:3072 + 1024 * a].rearrange("p (n c) -> p n c", n=2) for a in range(2)]

        ident = sb("ident", [P, P])
        ones = sb("ones", [P, P])
        before = reg_qg[:, 2 * D:2 * D + P]
        small = sb("small", [P, 606])
        at = [0]

        def take(n, parts=P):
            a = at[0]
            at[0] += n
            return small[0:parts, a:a + n]

        eps = take(1)
        lbw = take(4 * H).rearrange("p (a h) -> p a h", h=H)
        omlb = take(H)
        ngain = take(H)
        w00b = take(H)
        stat = take(72).rearrange("p (a n s) -> p a n s", a=3, s=6)
        mv = take(3 * 4).rearrange("p (a s) -> p a s", s=4)
        iota_cap = take(CAP)
        iota_i = take(CAP).bitcast(I32)
        back4 = take(EG)
        e64 = take(E)
        ecol = take(E)
        b64 = take(4)
        valid = take(3)
        fqk = take(3 * H * NS).rearrange("p (a h b) -> p a h b", a=3, b=NS)
        sel_at = take(3 * NITEM).rearrange("p (a i) -> p a i", i=NITEM)
        cw = take(6).rearrange("p (a w) -> p a w", w=2)
        rowi = take(6).rearrange("p (a w) -> p a w", w=2).bitcast(I32)
        plan = take(1 + NOV).bitcast(I32)
        pick = sb("pick", [P, 3, 2, CAP])

        rt = reg_pk
        rat = [KD * P]

        def rtake(n):
            a = rat[0]
            rat[0] += n
            return rt[:, a:a + n]

        def t3(n=E):
            return rtake(3 * n).rearrange("p (a e) -> p a e", a=3)

        rww = rtake(KD * E).rearrange("p (k e) -> p k e", e=E)
        rbw = rtake(E)
        probs, hot1, hot2, rest, sel, rank, ranked = (t3() for _ in range(7))
        best1, best2, gsum, tmp12 = (rtake(12).unsqueeze(2) for _ in range(4))
        hotg = t3(EG)
        r1 = t3(2)
        count, nmore, cum = (rtake(E) for _ in range(3))
        more, number, which, wtmp = (rtake(4 * E).rearrange("p (e b) -> p e b", b=4) for _ in range(4))
        pair16 = rtake(E * E).rearrange("p (e f) -> p e f", f=E)
        bm1 = rtake(4)
        evens = rtake(NOVP)
        planf = rtake(1 + NOV)
        assert rat[0] <= 2 * HT, rat

        osq = up[:, 2048:2048 + HT].rearrange("p (k t) -> p k t", t=T)
        ostd = up[:, 5120:5120 + HT].rearrange("p (k t) -> p k t", t=T)
        ks_rows = lngb[:, 0, :]

        def halves(buf, h, side):
            return buf[:, :, 0:NP_].rearrange("p k (b w x) -> p k b w x", w=2, x=h)[:, :, :, side, :]

        def total(buf, h, side):
            return halves(buf, h, side)[:, :, :, h - 1:h].broadcast_to([P, H, NP_ // (2 * h), h])

        psum = [ctx.enter_context(nc.psum_tensor(f"bank{b}", [P, 512], F32)) for b in range(8)]

        x_in = [sem(f"x_in{q}") for q in range(4)]; side_in = sem("side_in"); ln1_in = sem("ln1_in"); router_in = sem("router_in")
        landed = [sem(f"landed{s}") for s in range(8)]
        w_used = sem("w_used")
        consts = sem("consts"); pool_chain = sem("pool_chain")
        gemm = sem("gemm"); act_evac = sem("act_evac"); dve_evac = sem("dve_evac")
        lb_exp = sem("lb_exp"); lb_sub = sem("lb_sub")
        f_ready = sem("f_ready"); logf = sem("logf"); k_ready = sem("k_ready")
        i_tr = sem("i_tr"); i_ev = sem("i_ev"); v_tr = sem("v_tr"); v_ev = sem("v_ev")
        lvl_exp = sem("lvl_exp"); lvl_z = sem("lvl_z"); lvl_mm = sem("lvl_mm"); lvl_cp = sem("lvl_cp"); lvl_up = sem("lvl_up")
        kf_tr = sem("kf_tr"); kf_ev = sem("kf_ev"); st_mm = sem("st_mm"); st_ev = sem("st_ev")
        ks_tr = sem("ks_tr"); ks_ev = sem("ks_ev"); s0_in = [sem("s0_in0"), sem("s0_in1")]
        s_vd = sem("s_vd"); s_mm = sem("s_mm"); s_new = sem("s_new"); s_o = sem("s_o"); s_out = [sem("s_out0"), sem("s_out1")]
        o_mm = sem("o_mm"); o_ev = sem("o_ev"); vs_tr = sem("vs_tr"); sgu_mm = sem("sgu_mm"); sgu_ev = sem("sgu_ev")
        v_ln = sem("v_ln"); v_ln_var = sem("v_ln_var"); v_std = sem("v_std")
        o_sq = sem("o_sq"); n_mm = sem("n_mm"); n_std = sem("n_std"); yb_ready = sem("yb_ready"); ya_ready = sem("ya_ready")
        upper_free = sem("upper_free"); outs = sem("outs")
        h_tr = sem("h_tr"); h_ev = sem("h_ev"); l_var = sem("l_var"); l_std = sem("l_std"); l_inv = sem("l_inv"); x1s_ready = sem("x1s_ready"); x1_ready = sem("x1_ready")
        x_tr = sem("x_tr"); x_ev = sem("x_ev"); lg_mm = sem("lg_mm"); r_max = sem("r_max"); r_exp = sem("r_exp")
        sel_ready = sem("sel_ready"); rank_mm = sem("rank_mm"); plan_ready = sem("plan_ready"); rows_ready = sem("rows_ready")
        picked = sem("picked"); g_mm = sem("g_mm"); g_ev = sem("g_ev")
        silu = sem("silu"); hid_ready = sem("hid_ready"); hid_tr = sem("hid_tr"); hid_ev = sem("hid_ev")
        ob_ready = sem("ob_ready"); ob_free = sem("ob_free"); ob_out = [sem("ob_out0"), sem("ob_out1")]
        ln2_in = sem("ln2_in"); ax_ready = sem("ax_ready"); r_in = [[sem(f"r_in{t}{w}") for w in range(2)] for t in range(3)]; y_ready = sem("y_ready"); zeroed = sem("zeroed"); zero_out = sem("zero_out"); dve_chain = sem("dve_chain")

        I0, V0, U0, G0, GA0, GB0 = (start_of(s) for s in ("i", "v", "u", "g", "ga", "gb"))
        DIAG_AT = V0 + 3
        LEVEL_AT = [V0 + 5, V0 + 7, U0 + 1, U0 + 3, U0 + 5, U0 + 7, G0 + 1, G0 + 3]
        block = ctx.enter_context(nc.Block())

        def slot_of(c):
            return c % 4 if c < C_IN else (c - C_IN) % 8

        def uses_before(c):
            return sum(slot_of(d) == slot_of(c) for d in range(c))

        BASE_USES = [sum(slot_of(d) == s for d in range(C_ALL)) for s in range(8)]

        @block.sync
        def _(sp):
            def load_x(q):
                sp.dma_start(xt[:, 4 * q:4 * q + 4, :], x_t[4 * P * q:4 * P * (q + 1), :].rearrange("(k p) t -> p k t", p=P)).then_inc(x_in[q], 16)

            load_x(0)
            c = 0
            for name, first, tiles in GROUPS:
                for j in range(tiles // 2):
                    if c >= 4:
                        sp.wait_ge(w_used, c - 3)
                    col = (first + 2 * j) * P
                    sp.dma_start(ring[:, slot_of(c), :].rearrange("p (k n) -> p k n", k=KD),
                                 w_in[:, col:col + 2 * P].rearrange("(k p) n -> p k n", p=P)).then_inc(landed[slot_of(c)], 16)
                    if c == 0:
                        for q in range(1, 4):
                            load_x(q)
                    c += 1
            for j in range(4):
                for wt in (woa, wob):
                    if c < C_IN + 4:
                        sp.wait_ge(w_used, c - 3)
                    elif c == C_IN + 4:
                        sp.wait_ge(upper_free, 1)
                    sp.dma_start(ring[:, slot_of(c), :].rearrange("p (k n) -> p k n", k=H),
                                 wt[:, 512 * j:512 * (j + 1)].rearrange("(k p) n -> p k n", p=P)).then_inc(landed[slot_of(c)], 16)
                    c += 1
            for j in range(8):
                sp.wait_ge(w_used, c - 7)
                sp.dma_start(ring[:, slot_of(c), :].rearrange("p (k n) -> p k n", k=KD),
                             wo[:, 256 * j:256 * (j + 1)].rearrange("(k p) n -> p k n", p=P)).then_inc(landed[slot_of(c)], 16)
                c += 1

            def expert_pair(i, experts):
                for a in range(2):
                    for part, wt in enumerate((wg, wu, wd)):
                        for q in range(4):
                            m = 12 * a + 4 * part + q
                            s = m % 8
                            sp.wait_ge(w_used, i * UNITS + (C_ALL + m - 7))
                            rows = (FF if part == 2 else D) // 4
                            src = wt[experts[a], q * rows:(q + 1) * rows, :].rearrange("(k p) n -> p k n", p=P)
                            sp.dma_start(ring[:, s, :].rearrange("p (k n) -> p k n", k=rows // P), src).then_inc(landed[s], 16)

            with sp.Fori(0, NPAIR) as i:
                expert_pair(i, (i * 2, i * 2 + 1))
            sp.wait_ge(plan_ready, 1)
            pairs = sp.value_load(plan[0:1, 0:1], min_val=0, max_val=NOVP)
            with sp.If(pairs > 0):
                with sp.Fori(0, pairs) as j:
                    e0 = sp.value_load(plan[0:1, bass.ds(j * 2 + 1, 1)], min_val=0, max_val=E - 1)
                    e1 = sp.value_load(plan[0:1, bass.ds(j * 2 + 2, 1)], min_val=0, max_val=E - 1)
                    expert_pair(j + NPAIR, (e0, e1))
            sp.nop()

        @block.gpsimd
        def _(pool):
            n = [0]

            def link(ins):
                n[0] += 1
                ins.then_inc(pool_chain, 1)
                pool.wait_ge(pool_chain, n[0])

            with nc.allow_non_contiguous_dma("small parameters"):
                pool.dma_start(lbw[:, 0, :], lbl).then_inc(side_in, 16)
                pool.dma_start(ngain, normg).then_inc(side_in, 16)
                pool.dma_start(w00b, w00.partition_broadcast(P)).then_inc(side_in, 16)
                pool.dma_start(wsm, ws_t).then_inc(side_in, 16)
                pool.dma_start(bsb, b_s.partition_broadcast(P)).then_inc(side_in, 16)
                pool.dma_start(lngb[:, 0, :], lng.partition_broadcast(P)).then_inc(side_in, 16)
                pool.dma_start(lngb[:, 1, :], lnb.partition_broadcast(P)).then_inc(side_in, 16)
            link(pool.memset(ident[:, :], 0.0))
            link(pool.affine_select(out=ident[:, :], in_=ident[:, :], compare_op=ALU.not_equal, fill=1.0, base=0,
                                    pattern=[[-1, P]], channel_multiplier=1))
            pool.memset(ones[:, :], 1.0)
            pool.memset(eps, EPS)
            link(pool.memset(mask[:, :, :], 0.0))
            pool.affine_select(out=mask[:, 0, :], in_=mask[:, 0, :], compare_op=ALU.not_equal, fill=1.0, base=0,
                               pattern=[[-1, P]], channel_multiplier=1)
            for lv in range(7):
                h = 1 << lv
                pool.affine_select(out=mask[:, 1 + lv, :], in_=mask[:, 1 + lv, :], compare_op=ALU.is_ge, fill=1.0, base=0,
                                   pattern=[[-h, P // h], [0, h]], channel_multiplier=1)
            link(pool.memset(valid, 1.0))
            link(pool.affine_select(out=valid[:, 2:3], in_=valid[:, 2:3], compare_op=ALU.is_ge, fill=0.0, base=NS - 1,
                                    pattern=[[0, 1]], channel_multiplier=-1))
            for out, base, step, k in ((iota_cap, 0, 1, CAP), (back4, -EG, 1, EG), (e64, 0, CAP, E), (ecol, 0, 1, E), (b64, CAP, CAP, 4)):
                link(pool.iota(iota_i[:, 0:k], pattern=[[step, k]], base=base, channel_multiplier=0))
                link(pool.tensor_copy(out, iota_i[:, 0:k]))
            pool.wait_ge(zeroed, 1)
            for a in range(2):
                pool.dma_start(scratch[CAP * (E + 4 * a):CAP * (E + 4 * a + 4), :].rearrange("(p r) c -> p (r c)", p=P),
                               up[:, 0:4096]).then_inc(zero_out, 16)
            pool.wait_ge(side_in, 16 * 7)
            link(pool.affine_select(out=wsm, in_=wsm, compare_op=ALU.is_ge, fill=0.0, base=0,
                                    pattern=[[0, H], [1, P]], channel_multiplier=-1))
            pool.nop().then_inc(consts, 1)
            pool.wait_ge(st_ev, 1)
            pool.dma_start(st_p.rearrange("h k v -> k h v"), scum[:, :, 0:P]).then_inc(outs, 16)
            pool.wait_ge(v_ln, 3)
            pool.dma_start(v_s, vtm[0:NS, 2, :]).then_inc(outs, 16)
            for h in range(H):
                a = h % 2
                if h == 0:
                    pool.wait_ge(st_mm, 1)
                    for b in range(2):
                        pool.dma_start(s0b[b], state[:, b].rearrange("b k v -> k b v")).then_inc(s0_in[b], 16)
                pool.wait_ge(s_new, h + 1)
                pool.wait_ge(s_o, h + 1)
                pool.dma_start(st_s[:, h].rearrange("b k v -> k b v"), s0b[a]).then_inc(s_out[a], 16)
                if h + 2 < H:
                    pool.wait_ge(s_out[a], 16 * (h // 2 + 1))
                    pool.dma_start(s0b[a], state[:, h + 2].rearrange("b k v -> k b v")).then_inc(s0_in[a], 16)
            pool.wait_ge(w_used, C_IN + 8)
            pool.dma_start(lnp[:, 0, :], ln1g.partition_broadcast(P)).then_inc(ln1_in, 16)
            pool.dma_start(lnp[:, 1, :], ln1b.partition_broadcast(P)).then_inc(ln1_in, 16)
            link(pool.memset(before, 1.0))
            pool.affine_select(out=before, in_=before, compare_op=ALU.is_ge, fill=0.0, base=-1,
                               pattern=[[1, P]], channel_multiplier=-1).then_inc(consts, 1)
            pool.wait_ge(w_used, C_ALL)
            pool.dma_start(rww, rw.rearrange("(k p) e -> p k e", p=P)).then_inc(router_in, 16)
            pool.dma_start(rbw, rb.partition_broadcast(P)).then_inc(router_in, 16)
            pool.wait_ge(l_inv, 1)
            pool.wait_ge(ln1_in, 32)
            row = x1[0:NS, 2, :]
            link(pool.tensor_scalar(row, row, mv[0:NS, 2, 0:1], mv[0:NS, 2, 3:4], ALU.subtract, ALU.mult))
            link(pool.tensor_tensor(row, row, lnp[0:NS, 0, :], ALU.mult))
            pool.tensor_tensor(row, row, lnp[0:NS, 1, :], ALU.add).then_inc(x1s_ready, 1)
            pool.wait_ge(x1_ready, 2)
            pool.wait_ge(x1s_ready, 1)
            pool.dma_start(lnp[:, 0, :], ln2g.partition_broadcast(P)).then_inc(ln2_in, 16)
            pool.dma_start(lnp[:, 1, :], ln2b.partition_broadcast(P)).then_inc(ln2_in, 16)

            pool.sem_inc(ob_free, 2)

            def store_pair(i, rows):
                for a in range(2):
                    pool.wait_ge(ob_ready, i * 2 + (a + 2))
                    for half in range(2):
                        dst = scratch[bass.ds(rows + CAP * a, CAP), :].rearrange("s (n f c) -> f s n c", n=2, f=2)[half]
                        pool.dma_start(dst, ob[a][64 * half:64 * half + 64, :, :]).then_inc(ob_out[a], 16)
                    pool.wait_ge(ob_out[a], i * 32 + 32)
                    pool.sem_inc(ob_free, 1)

            with pool.Fori(0, NPAIR) as i:
                store_pair(i, i * (2 * CAP))
            pool.wait_ge(plan_ready, 1)
            pairs = pool.value_load(plan[0:1, 0:1], min_val=0, max_val=NOVP)
            with pool.If(pairs > 0):
                with pool.Fori(0, pairs) as j:
                    store_pair(j + NPAIR, (j + NPAIR) * (2 * CAP))
            pool.wait_ge(rows_ready, 1)
            pool.wait_ge(ob_free, 2 + E)
            for tt in (2, 0, 1):
                m = P if tt < 2 else NS
                for w in range(2):
                    pool.indirect_dma_start(out=ring[0:m, 2 * tt + w, 0:D], out_offset=None, in_=scratch[:, :],
                                            in_offset=bass.IndirectOffsetOnAxis(ap=rowi[0:m, tt, w:w + 1], axis=0)).then_inc(r_in[tt][w], 16)
            for n, tt in enumerate((2, 0, 1)):
                m = P if tt < 2 else NS
                pool.wait_ge(y_ready, n + 1)
                pool.dma_start(y[P * tt:P * tt + m, :], ring[0:m, 2 * tt, 0:D]).then_inc(outs, 16)
            pool.wait_ge(outs, 16 * 5)
            for a in range(2):
                pool.wait_ge(s_out[a], 16 * 4)

        @block.tensor
        def _(pe):
            ended = [False]

            def gemm_tile(n, slots_k, rhs, last_of_chunk):
                if n >= 4:
                    p = n - 4
                    if p < N_IN:
                        pe.wait_ge(act_evac, p + 1)
                    else:
                        pe.wait_ge(dve_evac, p - N_IN + 1)
                for k, lhs in enumerate(slots_k):
                    if n == 0 and k % 4 == 0:
                        pe.wait_ge(x_in[k // 4], 16)
                    mm = pe.matmul(psum[n % 4][:, 0:T], lhs, rhs[:, k, :], start=(k == 0), stop=(k == len(slots_k) - 1))
                    if k == 0 and ended[0]:
                        mm.then_inc(w_used, 1)
                mm.then_inc(gemm, 1)
                ended[0] = last_of_chunk

            def transposes(done, src, batch, evacuated):
                if batch:
                    pe.wait_ge(evacuated, 3)
                for tt in range(3):
                    m = P if tt < 2 else NS
                    for j in range(4):
                        mm = pe.transpose(psum[4 + tt][0:m, P * j:P * (j + 1)], src[:, 4 * batch + j, P * tt:P * tt + m], ident[:, :])
                    mm.then_inc(done, 1)

            def level(lv):
                if lv < 0:
                    a, b = kf, qf
                    pe.wait_ge(k_ready, 1)
                    pe.wait_ge(i_ev, 6)
                else:
                    a, b = z, z
                    pe.wait_ge(lvl_z, lv + 1)
                if lv == 7:
                    for h in range(H):
                        if h % 4 == 0:
                            pe.wait_ge(lvl_cp, 4 * 7 + h // 4 + 1)
                        mm = pe.matmul(psum[4 + h // 4][:, P * (h % 4):P * (h % 4 + 1)], z[:, h, 0:P], z[:, h, P:2 * P], start=True, stop=True)
                        if h % 4 == 3:
                            mm.then_inc(lvl_mm, 1)
                    return
                for r in range(4):
                    if lv == 1 and r < 3:
                        pe.wait_ge(v_ev, 3)
                    if lv == 2 and r < 3:
                        pe.wait_ge(v_ev, 6)
                    if lv >= 0:
                        pe.wait_ge(lvl_cp, 4 * lv + r + 1)
                    for j in range(4):
                        h, tt = 2 * r + j // 2, j % 2
                        mm = pe.matmul(psum[4 + r][:, P * j:P * (j + 1)], a[:, h, P * tt:P * tt + P], b[:, h, P * tt:P * tt + P], start=True, stop=True)
                    mm.then_inc(lvl_mm, 1)

            def v_transposes(batch):
                pe.wait_ge(act_evac, V0 + 4 * batch + 4)
                pe.wait_ge(lvl_cp, 4 * (2 if batch == 0 else 3))
                for tt in range(3):
                    m = P if tt < 2 else NS
                    for j in range(4):
                        mm = pe.transpose(psum[4 + tt][0:m, P * j:P * (j + 1)], vi[:, 4 * batch + j, P * tt:P * tt + m], ident[:, :])
                    mm.then_inc(v_tr, 1)

            def side(n):
                if n == I0 + 5:
                    pe.wait_ge(consts, 1)
                    pe.wait_ge(act_evac, I0 + 4)
                    transposes(i_tr, vi, 0, i_ev)
                if n == V0:
                    pe.wait_ge(act_evac, I0 + 8)
                    transposes(i_tr, vi, 1, i_ev)
                if n == DIAG_AT:
                    level(-1)
                if n in LEVEL_AT:
                    level(LEVEL_AT.index(n))
                if n == V0 + 6:
                    v_transposes(0)
                if n == U0 + 0:
                    v_transposes(1)
                if n == G0 + 5:
                    pe.wait_ge(kf_ev, 1)
                    for r in range(4):
                        if r < 2:
                            pe.wait_ge(lvl_cp, 4 * 8 + r + 1)
                        for j in range(4):
                            mm = pe.transpose(psum[4 + r][:, P * j:P * (j + 1)], z[:, 4 * (r % 2) + j, P * (r // 2):P * (r // 2) + P], ident[:, :])
                        mm.then_inc(kf_tr, 1)
                if n == G0 + 7:
                    for r in range(2):
                        pe.wait_ge(kf_ev, 5)
                        for j in range(4):
                            h = 4 * r + j
                            for tt in range(2):
                                mm = pe.matmul(psum[4 + r][:, P * j:P * (j + 1)], ktm[:, tt, P * h:P * h + P], itm[:, tt, P * h:P * h + P],
                                               start=(tt == 0), stop=(tt == 1))
                    mm.then_inc(st_mm, 1)
                    for r in range(2):
                        for j in range(4):
                            mm = pe.transpose(psum[6 + r][0:NS, P * j:P * (j + 1)], fqk[:, 2, 4 * r + j, :], ident[:, :])
                    mm.then_inc(ks_tr, 1)
                if GA0 <= n < GA0 + 8:
                    h = n - GA0
                    pe.wait_ge(ks_ev, 1)
                    pe.wait_ge(st_ev, 1)
                    pe.wait_ge(s_vd, h + 1)
                    for r in range(2):
                        if h:
                            pe.wait_ge(s_new, h)
                        mm = pe.matmul(psum[4 + r][:, :], ks_rows[0:NS, P * h:P * h + P], vdb[h % 2][:, 4 * r:4 * r + 4, :], start=True, stop=True)
                    mm.then_inc(s_mm, 1)
                    if h:
                        sample_out(h - 1)
                if n == GA0 + 8:
                    sample_out(7)
                if GA0 + 9 <= n < GA0 + 13:
                    for h in (2 * (n - GA0 - 9), 2 * (n - GA0 - 9) + 1):
                        b = psum[(4, 5, 7)[h % 3]]
                        if h >= 3:
                            pe.wait_ge(o_ev, h - 2)
                        else:
                            pe.wait_ge(s_new, 8)
                            pe.wait_ge(ks_ev, 1)
                        pe.matmul(b[:, 0:P], itm[:, 0, P * h:P * h + P], sc[:, h, 0, :], start=True, stop=True)
                        pe.matmul(b[:, P:2 * P], itm[:, 0, P * h:P * h + P], scx[:, h, :], start=True, stop=False)
                        pe.matmul(b[:, P:2 * P], itm[:, 1, P * h:P * h + P], sc[:, h, 1, :], start=False, stop=True).then_inc(o_mm, 1)
                if n == GA0 + 13:
                    pe.wait_ge(v_ln, 3)
                    pe.wait_ge(o_ev, 9)
                    for g in range(H):
                        mm = pe.transpose(psum[6][:, NS * g:NS * (g + 1)], vtm[0:NS, 2, P * g:P * g + P], ident[0:NS, 0:NS])
                    mm.then_inc(vs_tr, 1)
                if GA0 + 13 <= n < GA0 + 17:
                    for g in (2 * (n - GA0 - 13), 2 * (n - GA0 - 13) + 1):
                        b = psum[(4, 5, 7)[g % 3]]
                        if g >= 3:
                            pe.wait_ge(sgu_ev, g - 2)
                        else:
                            pe.wait_ge(o_ev, 9)
                        for tt in range(2):
                            mm = pe.matmul(b[:, P * tt:P * tt + P], vtm[:, tt, P * g:P * g + P], wsm[:, g, :], start=True, stop=True)
                        mm.then_inc(sgu_mm, 1)
                if n == GB0 + 3:
                    for h in range(H):
                        b = psum[4 + h % 4]
                        if h >= 4:
                            pe.wait_ge(n_std, h - 3)
                        else:
                            pe.wait_ge(sgu_ev, 9)
                            pe.wait_ge(o_sq, 1)
                        pe.matmul(b[:, 0:T], ones[:, :], osq[:, h, :], start=True, stop=True).then_inc(n_mm, 1)

            def sample_out(h):
                pe.wait_ge(s_new, h + 1)
                for b in range(NS):
                    mm = pe.matmul(psum[6][:, NS * h + b:NS * h + b + 1], s0b[h % 2][:, b, :], fqk[:, 1, h, b:b + 1], start=True, stop=True)
                mm.then_inc(s_o, 1)

            for n in range(N_IN):
                c = n // 2
                if n % 2 == 0:
                    pe.wait_ge(landed[slot_of(c)], 16 * (uses_before(c) + 1))
                wt = ring[:, slot_of(c), :].rearrange("p (k n) -> p k n", k=KD)
                gemm_tile(n, [wt[:, k, P * (n % 2):P * (n % 2) + P] for k in range(KD)], xt, n % 2 == 1)
                side(n)
            for j in range(KD):
                for br, src in ((0, u), (1, qf)):
                    c = C_IN + 2 * (j // 4) + br
                    n = N_IN + 2 * j + br
                    if j % 4 == 0:
                        pe.wait_ge(landed[slot_of(c)], 16 * (uses_before(c) + 1))
                    if j == 0:
                        pe.wait_ge((ya_ready, yb_ready)[br], 1)
                    wt = ring[:, slot_of(c), :].rearrange("p (k n) -> p k n", k=H)
                    gemm_tile(n, [wt[:, k, P * (j % 4):P * (j % 4) + P] for k in range(H)], src, j % 4 == 3)

            def to_tm(batch):
                pe.wait_ge(dve_evac, N_OUT + 4 * batch + 4)
                for tt in range(3):
                    m = P if tt < 2 else NS
                    if batch:
                        pe.wait_ge(h_ev, 3 * (batch - 1) + tt + 1)
                    for j in range(4):
                        mm = pe.transpose(psum[4 + tt][0:m, P * j:P * (j + 1)], xt[:, 4 * batch + j, P * tt:P * tt + m], ident[:, :])
                        if batch == 3 and tt == 0 and j == 0:
                            mm.then_inc(w_used, 1)
                    mm.then_inc(h_tr, 1)

            for j in range(KD):
                n = N_IN + N_OUT + j
                c = C_IN + 8 + j // 2
                if j % 2 == 0:
                    pe.wait_ge(landed[slot_of(c)], 16 * (uses_before(c) + 1))
                if j == 0:
                    pe.wait_ge(dve_evac, N_OUT)
                wt = ring[:, slot_of(c), :].rearrange("p (k n) -> p k n", k=KD)
                gemm_tile(n, [wt[:, k, P * (j % 2):P * (j % 2) + P] for k in range(KD)], ga, j % 2 == 1)
                if j % 4 == 1 and j > 4:
                    to_tm(j // 4 - 1)
            to_tm(3)
            pe.wait_ge(dve_evac, N_OUT + KD)
            pe.wait_ge(h_ev, 12)
            for tt in range(3):
                m = P if tt < 2 else NS
                pe.wait_ge(x1_ready if tt < 2 else x1s_ready, tt + 1 if tt < 2 else 1)
                for r in range(4):
                    if tt:
                        pe.wait_ge(x_ev, 4 * (tt - 1) + r + 1)
                    for j in range(4):
                        k = 4 * r + j
                        mm = pe.transpose(psum[r][:, m * j:m * (j + 1)], x1[0:m, tt, P * k:P * k + P], ident[0:m, 0:m])
                    mm.then_inc(x_tr, 1)
                if tt == 0:
                    pe.wait_ge(router_in, 32)
                pe.wait_ge(x_ev, 4 * tt + 4)
                for k in range(KD):
                    mm = pe.matmul(psum[4][0:m, E * tt:E * (tt + 1)], xt[:, k, P * tt:P * tt + m], rww[:, k, :], start=(k == 0), stop=(k == KD - 1))
            mm.then_inc(lg_mm, 1)
            pe.wait_ge(sel_ready, 1)
            pe.wait_ge(consts, 2)
            for tt in range(3):
                for s in range(tt):
                    pe.matmul(psum[5][:, E * tt:E * (tt + 1)], ones[:, :], sel[:, s, :], start=(s == 0), stop=False)
                pe.matmul(psum[5][:, E * tt:E * (tt + 1)], before[:, :], sel[:, tt, :], start=(tt == 0), stop=True)
            for s in range(3):
                mm = pe.matmul(psum[5][:, 3 * E:4 * E], ones[:, :], sel[:, s, :], start=(s == 0), stop=(s == 2))
            mm.then_inc(rank_mm, 1)

            def gather(p):
                pe.wait_ge(picked, p + 1)
                for r in range(4):
                    b = psum[7 - r % 2]
                    pe.wait_ge(g_ev, p * 4 + (r + 1))
                    for j in range(4):
                        for tt in range(3):
                            k = 4 * r + j
                            mm = pe.matmul(b[:, P * j:P * (j + 1)], x1[:, tt, P * k:P * k + P],
                                           pick[:, tt, :, :].rearrange("p a s -> p (a s)"), start=(tt == 0), stop=(tt == 2))
                    mm.then_inc(g_mm, 1)

            def unit(i, m):
                pe.wait_ge(landed[m % 8], i * 48 + 16 * (BASE_USES[m % 8] + m // 8 + 1))
                return ring[:, m % 8, :]

            def expert(i, a):
                gate, upb = psum[2 * a], psum[2 * a + 1]
                if a == 0:
                    pe.wait_ge(g_ev, i * 4 + 6)
                for part, bank in ((0, gate), (1, upb)):
                    for q in range(4):
                        wt = unit(i, 12 * a + 4 * part + q).rearrange("p (k n) -> p k n", k=4)
                        for kk in range(4):
                            k = 4 * q + kk
                            for half in range(2):
                                mm = pe.matmul(bank[64 * half:64 * half + 64, :], xg[:, k, CAP * a:CAP * a + CAP],
                                               wt[:, kk, 512 * half:512 * half + 512], start=(k == 0), stop=(k == KD - 1))
                        mm.then_inc(w_used, 1)

            def down(i, a):
                pe.wait_ge(hid_ready, i * 2 + (a + 1))
                if a:
                    pe.wait_ge(g_ev, i * 4 + 10)
                for j in range(4):
                    mm = pe.transpose(psum[6][:, P * j:P * (j + 1)], hid[a][:, P * j:P * (j + 1)], ident[:, :])
                mm.then_inc(hid_tr, 1)
                pe.wait_ge(hid_ev, i * 2 + (a + 1))
                pe.wait_ge(ob_ready, i * 2 + (a + 1))
                for q in range(4):
                    wt = unit(i, 12 * a + 8 + q).rearrange("p (k n) -> p k n", k=2)
                    for kk in range(2):
                        k = 2 * q + kk
                        for nn in range(4):
                            mm = pe.matmul(psum[4 + nn // 2][64 * (nn % 2):64 * (nn % 2) + 64, :], hidt[a][:, k % 4, k // 4, :],
                                           wt[:, kk, 512 * nn:512 * nn + 512], start=(k == 0), stop=(k == 7))
                    mm.then_inc(w_used, 1)

            def pair(i):
                expert(i, 0)
                down(i, 0)
                expert(i, 1)
                gather(i + 1)
                down(i, 1)

            gather(0)
            with pe.Fori(0, NPAIR) as i:
                pair(i)
            pe.wait_ge(plan_ready, 1)
            pairs = pe.value_load(plan[0:1, 0:1], min_val=0, max_val=NOVP)
            with pe.If(pairs > 0):
                with pe.Fori(0, pairs) as j:
                    pair(j + NPAIR)
            pe.nop()

        @block.scalar
        def _(act):
            evac_of = {}
            n = 0
            for name, _, tiles in GROUPS:
                for j in range(tiles):
                    evac_of[n] = (name, j)
                    n += 1
            act.wait_ge(consts, 1)
            act.wait_ge(lb_sub, 1)
            act.activation(lbw[:, 1, :], lbw[:, 1, :], ACT.Exp).then_inc(lb_exp, 1)

            def exps(lv):
                if lv:
                    act.wait_ge(lvl_mm, 4 * (lv + 1))
                    act.wait_ge(lvl_up, lv)
                else:
                    act.wait_ge(logf, 1)
                    act.wait_ge(zeroed, 1)
                h = 1 << lv
                act.activation(halves(z, h, 1), halves(pcum, h, 1), ACT.Exp).then_inc(lvl_exp, 1)
                act.activation(halves(z, h, 0), halves(scum, h, 0), ACT.Exp).then_inc(lvl_exp, 1)

            func = {"q": ACT.Silu, "i": ACT.Copy, "v": ACT.Gelu_apprx_tanh, "u": ACT.Gelu_apprx_tanh, "g": ACT.Silu,
                    "ga": ACT.Sigmoid, "gb": ACT.Sigmoid}
            dest = {"q": qf, "i": vi, "v": vi, "u": u, "g": gf, "ga": ga, "gb": gb}
            for n in range(N_IN):
                name, j = evac_of[n]
                act.wait_ge(gemm, n + 1)
                src = psum[n % 4][:, 0:T]
                if name == "f":
                    act.activation(pcum[:, j, :], src, ACT.Sigmoid)
                    act.activation(kf[:, j, :], src, ACT.Sigmoid, scale=-1.0).then_inc(act_evac, 1)
                else:
                    if name == "v" and j == 0:
                        act.wait_ge(i_tr, 6)
                    if name == "ga" and j == 0:
                        act.wait_ge(st_mm, 1)
                    if name == "gb" and j == 0:
                        act.wait_ge(s_o, 8)
                        act.wait_ge(s_out[0], 64)
                        act.wait_ge(s_out[1], 64)
                    act.activation(dest[name][:, j, :], src, func[name]).then_inc(act_evac, 1)
                if name == "q" and j == 3:
                    act.wait_ge(f_ready, 1)
                    act.activation(pcum[:, :, 0:NP_], pcum[:, :, 0:NP_], ACT.Ln).then_inc(logf, 1)
                if n == V0 + 3:
                    exps(0)
                if n in LEVEL_AT[:-1]:
                    exps(LEVEL_AT.index(n) + 1)
                if n == G0 + 3:
                    act.wait_ge(lvl_mm, 34)
                    act.wait_ge(lvl_up, 8)
                    act.activation(z, scum, ACT.Exp).then_inc(lvl_exp, 1)
                if n == U0 + 3:
                    for tt in range(3):
                        m = P if tt < 2 else NS
                        act.wait_ge(v_ln_var, tt + 1)
                        act.activation(mv[0:m, tt, 2:3], mv[0:m, tt, 1:2], ACT.Sqrt, bias=eps[0:m, :]).then_inc(v_std, 1)
                if n == GA0 + 14:
                    act.wait_ge(o_ev, 9)
                    act.activation(osq[:, :, :], qf[:, :, :], ACT.Square).then_inc(o_sq, 1)
                if n == GB0 + 3:
                    for h in range(H):
                        act.wait_ge(n_mm, h + 1)
                        act.activation(ostd[:, h, :], psum[4 + h % 4][:, 0:T], ACT.Sqrt, bias=eps, scale=1.0 / P).then_inc(n_std, 1)
            act.wait_ge(l_var, 1)
            act.activation(mv[:, :, 2], mv[:, :, 1], ACT.Sqrt, bias=eps).then_inc(l_std, 1)
            for tt in range(3):
                m = P if tt < 2 else NS
                for r in range(4):
                    act.wait_ge(x_tr, 4 * tt + r + 1)
                    act.copy(xt[:, 4 * r:4 * r + 4, P * tt:P * tt + m], psum[r][:, 0:4 * m].rearrange("p (k t) -> p k t", t=m)).then_inc(x_ev, 1)
            act.wait_ge(r_max, 1)
            act.activation(probs, probs, ACT.Exp).then_inc(r_exp, 1)

            def pair(i):
                for a in range(2):
                    act.wait_ge(w_used, i * UNITS + (C_ALL + 12 * a + 8))
                    act.activation(hid[a], psum[2 * a][:, :], ACT.Silu).then_inc(silu, 1)
                    act.wait_ge(hid_tr, i * 2 + (a + 1))
                    act.copy(hidt[a].rearrange("p j f s -> p (j f s)"), psum[6][:, :]).then_inc(hid_ev, 1)

            with act.Fori(0, NPAIR) as i:
                pair(i)
            act.wait_ge(plan_ready, 1)
            pairs = act.value_load(plan[0:1, 0:1], min_val=0, max_val=NOVP)
            with act.If(pairs > 0):
                with act.Fori(0, pairs) as j:
                    pair(j + NPAIR)
            for tt in range(3):
                m = P if tt < 2 else NS
                act.mul(x1[0:m, tt, :], x1[0:m, tt, :], ALPHA).then_inc(ax_ready, 1)
            for n, tt in enumerate((2, 0, 1)):
                m = P if tt < 2 else NS
                act.wait_ge(l_var, n + 2)
                act.activation(mv[0:m, tt, 2:3], mv[0:m, tt, 1:2], ACT.Sqrt, bias=eps[0:m, :]).then_inc(l_std, 1)

        @block.vector
        def _(dve):
            chain = [0]

            def link(ins):
                chain[0] += 1
                ins.then_inc(dve_chain, 1)
                dve.wait_ge(dve_chain, chain[0])

            def normalise(row, tt, m, done):
                link(dve.scalar_tensor_tensor(out=row, in0=row, scalar=mv[0:m, tt, 0:1], in1=lnp[0:m, 0, :],
                                              op0=ALU.subtract, op1=ALU.mult))
                dve.scalar_tensor_tensor(out=row, in0=row, scalar=mv[0:m, tt, 3:4], in1=lnp[0:m, 1, :],
                                         op0=ALU.mult, op1=ALU.add).then_inc(done, 1)

            dve.memset(up[:, 0:4096], 0.0).then_inc(zeroed, 1)
            dve.wait_ge(side_in, 16 * 7)
            dve.wait_ge(consts, 1)
            dve.tensor_tensor(lbw[:, 1, :], lbw[:, 0, :], lbw[:, 0, :], ALU.subtract).then_inc(lb_sub, 1)
            dve.wait_ge(lb_exp, 1)
            link(dve.reciprocal(lbw[:, 2, :], lbw[:, 1, :]))
            link(dve.tensor_tensor(lbw[:, 2, :], lbw[:, 1, :], lbw[:, 2, :], ALU.mult))
            link(dve.tensor_tensor(lbw[:, 3, :], lbw[:, 2, :], lbw[:, 2, :], ALU.subtract))
            link(dve.tensor_scalar(omlb, lbw[:, 3, :], -1.0, 1.0, ALU.mult, ALU.add))
            for h in range(H):
                dve.wait_ge(act_evac, h + 1)
                dve.tensor_scalar(pcum[:, h, :], pcum[:, h, :], omlb[:, h:h + 1], lbw[:, 3, h:h + 1], ALU.mult, ALU.add)
                ins = dve.tensor_scalar(kf[:, h, :], kf[:, h, :], omlb[:, h:h + 1], None, ALU.mult)
            link(ins)
            link(dve.tensor_copy(fqk[:, 0, :, :], pcum[:, :, NP_:T]))
            dve.tensor_copy(fqk[:, 2, :, :], kf[:, :, NP_:T]).then_inc(f_ready, 1)
            dve.wait_ge(act_evac, 16)
            dve.tensor_copy(fqk[:, 1, :, :], qf[:, :, NP_:T]).then_inc(k_ready, 1)

            def evac_tm(tr, ev, dst, batch):
                for tt in range(3):
                    m = P if tt < 2 else NS
                    dve.wait_ge(tr, 3 * batch + tt + 1)
                    dve.tensor_copy(dst[0:m, tt, 512 * batch:512 * batch + 512], psum[4 + tt][0:m, :]).then_inc(ev, 1)

            evac_tm(i_tr, i_ev, itm, 0)
            evac_tm(i_tr, i_ev, itm, 1)

            def copies(lv):
                if lv == 7:
                    for r in range(2):
                        dve.wait_ge(lvl_mm, 4 * 8 + r + 1)
                        dve.tensor_copy(scx[:, 4 * r:4 * r + 4, :], psum[4 + r][:, :].rearrange("p (h t) -> p h t", t=P)).then_inc(lvl_cp, 1)
                    return
                for r in range(4):
                    dve.wait_ge(lvl_mm, 4 * (lv + 1) + r + 1)
                    dve.copy_predicated(sc[:, 2 * r:2 * r + 2, :, :].rearrange("p h a t -> p (h a) t"),
                                        mask[:, lv + 1:lv + 2, :].bitcast(I32).broadcast_to([P, 4, P]),
                                        psum[4 + r][:, :].rearrange("p (h t) -> p h t", t=P)).then_inc(lvl_cp, 1)
                dve.wait_ge(lvl_cp, 4 * (lv + 2))

            def decay(lv):
                h = 1 << lv
                dve.wait_ge(lvl_exp, 2 * lv + 2)
                dve.tensor_tensor(halves(z, h, 1), halves(z, h, 1), halves(qf, h, 1), ALU.mult)
                dve.tensor_tensor(halves(z, h, 0), halves(z, h, 0), halves(kf, h, 0), ALU.mult).then_inc(lvl_z, 1)
                link(dve.tensor_tensor(halves(scum, h, 0), halves(scum, h, 0), total(pcum, h, 1), ALU.add))
                dve.tensor_tensor(halves(pcum, h, 1), halves(pcum, h, 1), total(pcum, h, 0), ALU.add).then_inc(lvl_up, 1)
                dve.wait_ge(lvl_up, lv + 1)

            dve.wait_ge(zero_out, 32)
            copies(-1)
            decay(0)
            copies(0)
            evac_tm(v_tr, v_ev, vtm, 0)
            decay(1)
            copies(1)
            evac_tm(v_tr, v_ev, vtm, 1)
            decay(2)
            copies(2)
            dve.wait_ge(v_ev, 6)
            for tt in range(3):
                m = P if tt < 2 else NS
                row = vtm[0:m, tt, :]
                for j in range(2):
                    ins = dve.bn_stats(stat[0:m, tt, j, :], row[:, 512 * j:512 * j + 512])
                link(ins)
                dve.bn_aggr(mv[0:m, tt, 0:2], stat[0:m, tt, 0:2, :].rearrange("p n s -> p (n s)")).then_inc(v_ln_var, 1)
                dve.wait_ge(v_ln_var, tt + 1)
            decay(3)
            copies(3)
            for tt in range(3):
                m = P if tt < 2 else NS
                row = vtm[0:m, tt, :]
                dve.wait_ge(v_std, tt + 1)
                link(dve.reciprocal(mv[0:m, tt, 3:4], mv[0:m, tt, 2:3]))
                link(dve.tensor_scalar(row, row, mv[0:m, tt, 0:1], mv[0:m, tt, 3:4], ALU.subtract, ALU.mult))
                link(dve.tensor_tensor(row, row, lngb[0:m, 0, :], ALU.mult))
                dve.tensor_tensor(row, row, lngb[0:m, 1, :], ALU.add).then_inc(v_ln, 1)
            for lv in range(4, 8):
                decay(lv)
                copies(lv)
            dve.wait_ge(lvl_exp, 17)
            dve.tensor_tensor(z, z, kf[:, :, 0:NP_], ALU.mult).then_inc(kf_ev, 1)
            for r in range(4):
                dve.wait_ge(kf_tr, r + 1)
                dve.tensor_copy(ktm[:, r // 2, 512 * (r % 2):512 * (r % 2) + 512], psum[4 + r][:, :]).then_inc(kf_ev, 1)
            dve.wait_ge(st_mm, 1)
            for r in range(2):
                ins = dve.tensor_copy(scum[:, 4 * r:4 * r + 4, 0:P], psum[4 + r][:, :].rearrange("p (h v) -> p h v", v=P))
            ins.then_inc(st_ev, 1)
            dve.wait_ge(ks_tr, 1)
            for r in range(2):
                ins = dve.tensor_copy(ks_rows[0:NS, 512 * r:512 * r + 512], psum[6 + r][0:NS, :])
            ins.then_inc(ks_ev, 1)
            for h in range(H):
                a = h % 2
                if h >= 2:
                    dve.wait_ge(s_mm, h - 1)
                dve.tensor_tensor(vdb[a], itm[0:NS, 2:3, P * h:P * h + P].broadcast_to([NS, NS, P]),
                                  ident[0:NS, 0:NS].unsqueeze(2).broadcast_to([NS, NS, P]), ALU.mult).then_inc(s_vd, 1)
                dve.wait_ge(s0_in[a], 16 * (h // 2 + 1))
                link(dve.tensor_tensor(s0b[a], s0b[a], fqk[:, 0, h, :].unsqueeze(2).broadcast_to([P, NS, P]), ALU.mult))
                dve.wait_ge(s_mm, h + 1)
                for r in range(2):
                    ins = dve.tensor_tensor(s0b[a][:, 4 * r:4 * r + 4, :], s0b[a][:, 4 * r:4 * r + 4, :],
                                            psum[4 + r][:, :].rearrange("p (b v) -> p b v", v=P), ALU.add)
                ins.then_inc(s_new, 1)
            for h in range(H):
                dve.wait_ge(o_mm, h + 1)
                dve.tensor_copy(qf[:, h, 0:NP_], psum[(4, 5, 7)[h % 3]][:, 0:NP_]).then_inc(o_ev, 1)
            dve.wait_ge(s_o, 8)
            dve.tensor_copy(qf[:, :, NP_:T], psum[6][:, 0:H * NS].rearrange("p (h b) -> p h b", b=NS)).then_inc(o_ev, 1)
            dve.wait_ge(act_evac, U0 + 8)
            for g in range(H):
                b = psum[(4, 5, 7)[g % 3]][:, 0:NP_].rearrange("p (a t) -> p a t", t=P)
                dve.wait_ge(sgu_mm, g + 1)
                link(dve.tensor_tensor(b, b, bsb[:, g:g + 1, :].broadcast_to([P, 2, P]), ALU.add))
                ug = u[:, g, 0:NP_].rearrange("p (a t) -> p a t", t=P)
                dve.tensor_tensor(ug, ug, b, ALU.mult).then_inc(sgu_ev, 1)
            dve.wait_ge(vs_tr, 1)
            vs = psum[6][:, 0:H * NS].rearrange("p (g b) -> p g b", b=NS)
            link(dve.tensor_tensor(vs, vs, w00b.unsqueeze(2).broadcast_to([P, H, NS]), ALU.mult))
            link(dve.tensor_tensor(vs, vs, bsb[:, :, 0:1].broadcast_to([P, H, NS]), ALU.add))
            dve.tensor_tensor(u[:, :, NP_:T], u[:, :, NP_:T], vs, ALU.mult).then_inc(sgu_ev, 1)
            dve.wait_ge(sgu_ev, 9)
            dve.nop().then_inc(ya_ready, 1)
            for h in range(H):
                dve.wait_ge(n_std, h + 1)
            link(dve.reciprocal(ostd[:, :, :], ostd[:, :, :]))
            for h in range(H):
                ins = dve.scalar_tensor_tensor(out=qf[:, h, :], in0=qf[:, h, :], scalar=ngain[:, h:h + 1], in1=ostd[:, h, :],
                                               op0=ALU.mult, op1=ALU.mult)
            link(ins)
            dve.tensor_tensor(qf[:, :, :], qf[:, :, :], gf[:, :, :], ALU.mult).then_inc(yb_ready, 1)
            dve.wait_ge(yb_ready, 1)
            dve.wait_ge(outs, 32)
            dve.nop().then_inc(upper_free, 1)
            for j in range(KD):
                n = N_IN + 2 * j
                dve.wait_ge(act_evac, N_IN)
                dve.wait_ge(gemm, n + 1)
                dve.tensor_tensor(ga[:, j, :], ga[:, j, :], psum[n % 4][:, 0:T], ALU.mult).then_inc(dve_evac, 1)
                dve.wait_ge(gemm, n + 2)
                link(dve.tensor_tensor(gb[:, j, :], gb[:, j, :], psum[(n + 1) % 4][:, 0:T], ALU.mult))
                dve.tensor_tensor(ga[:, j, :], ga[:, j, :], gb[:, j, :], ALU.add).then_inc(dve_evac, 1)

            def h_tm(batch):
                for tt in range(3):
                    m = P if tt < 2 else NS
                    dve.wait_ge(h_tr, 3 * batch + tt + 1)
                    dve.bn_stats(stat[0:m, tt, batch, :], psum[4 + tt][0:m, :])
                    dve.tensor_copy(x1[0:m, tt, 512 * batch:512 * batch + 512], psum[4 + tt][0:m, :]).then_inc(h_ev, 1)

            for j in range(KD):
                n = N_IN + N_OUT + j
                dve.wait_ge(gemm, n + 1)
                if j == 0:
                    link(dve.memset(x1[:, 2, :], 0.0))
                dve.scalar_tensor_tensor(out=xt[:, j, :], in0=xt[:, j, :], scalar=ALPHA, in1=psum[n % 4][:, 0:T],
                                         op0=ALU.mult, op1=ALU.add).then_inc(dve_evac, 1)
                if j % 4 == 1 and j > 4:
                    h_tm(j // 4 - 1)
            link(dve.memset(mv, 1.0))
            h_tm(3)
            dve.wait_ge(h_ev, 12)
            for tt in range(3):
                m = P if tt < 2 else NS
                ins = dve.bn_aggr(mv[0:m, tt, 0:2], stat[0:m, tt, :, :].rearrange("p n s -> p (n s)"))
            ins.then_inc(l_var, 1)
            dve.wait_ge(l_std, 1)
            dve.reciprocal(mv[:, :, 3], mv[:, :, 2]).then_inc(l_inv, 1)
            dve.wait_ge(l_inv, 1)
            dve.wait_ge(ln1_in, 32)
            for tt in range(2):
                normalise(x1[:, tt, :], tt, P, x1_ready)

            link(dve.memset(probs, 0.0))
            dve.memset(sel_at, -1.0)
            dve.wait_ge(lg_mm, 1)
            dve.wait_ge(router_in, 32)
            for tt in range(3):
                m = P if tt < 2 else NS
                ins = dve.tensor_tensor(probs[0:m, tt, :], psum[4][0:m, E * tt:E * (tt + 1)], rbw[0:m, :], ALU.add)
            link(ins)
            link(dve.tensor_reduce(r1[:, :, 0:1], probs, AX.X, ALU.max))
            dve.tensor_tensor(probs, probs, r1[:, :, 0:1].broadcast_to([P, 3, E]), ALU.subtract).then_inc(r_max, 1)
            dve.wait_ge(r_exp, 1)
            link(dve.tensor_reduce(r1[:, :, 0:1], probs, AX.X, ALU.add))
            link(dve.reciprocal(r1[:, :, 0:1], r1[:, :, 0:1]))
            link(dve.tensor_tensor(probs, probs, r1[:, :, 0:1].broadcast_to([P, 3, E]), ALU.mult))

            def flat(a):
                return a.rearrange("p a (g e) -> p (a g) e", e=EG)

            def first_max(src, best, hot, tmp, n):
                link(dve.tensor_reduce(best, src, AX.X, ALU.max))
                link(dve.tensor_tensor(hot, src, best.broadcast_to([P, n, EG]), ALU.is_equal))
                link(dve.tensor_tensor(hot, hot, back4.unsqueeze(1).broadcast_to([P, n, EG]), ALU.mult))
                link(dve.tensor_reduce(tmp, hot, AX.X, ALU.min))
                link(dve.tensor_tensor(hot, tmp.broadcast_to([P, n, EG]), back4.unsqueeze(1).broadcast_to([P, n, EG]), ALU.is_equal))

            first_max(flat(probs), best1, flat(hot1), tmp12, 12)
            link(dve.scalar_tensor_tensor(out=rest, in0=hot1, scalar=-2.0, in1=probs, op0=ALU.mult, op1=ALU.add))
            first_max(flat(rest), best2, flat(hot2), tmp12, 12)
            link(dve.tensor_tensor(gsum, best1, best2, ALU.add))
            g3 = gsum.rearrange("p (a g) o -> p a (g o)", a=3)
            first_max(g3, r1[:, :, 0:1], hotg, r1[:, :, 1:2], 3)
            hg = hotg.rearrange("p a g -> p (a g)").unsqueeze(2)
            for hot, best, w in ((hot1, best1, 0), (hot2, best2, 1)):
                dve.tensor_tensor(flat(hot), flat(hot), hg.broadcast_to([P, 12, EG]), ALU.mult)
                link(dve.tensor_tensor(best, best, hg, ALU.mult))
                link(dve.tensor_reduce(cw[:, :, w:w + 1], best.rearrange("p (a g) o -> p a (g o)", a=3), AX.X, ALU.add))
            link(dve.tensor_reduce(r1[:, :, 0:1], cw, AX.X, ALU.add))
            link(dve.reciprocal(r1[:, :, 0:1], r1[:, :, 0:1]))
            dve.tensor_tensor(cw, cw, r1[:, :, 0:1].broadcast_to([P, 3, 2]), ALU.mult)
            link(dve.tensor_tensor(sel, hot1, hot2, ALU.add))
            dve.tensor_tensor(sel, sel, valid.unsqueeze(2).broadcast_to([P, 3, E]), ALU.mult).then_inc(sel_ready, 1)
            dve.wait_ge(sel_ready, 1)
            dve.wait_ge(rank_mm, 1)
            link(dve.tensor_copy(rank.rearrange("p a e -> p (a e)"), psum[5][:, 0:3 * E]))
            link(dve.tensor_copy(count, psum[5][:, 3 * E:4 * E]))
            link(dve.tensor_scalar(ranked, rank, FAR, None, ALU.add))
            link(dve.tensor_tensor(ranked, ranked, sel, ALU.mult))
            def choose(p):
                dve.tensor_tensor(pick[:, :, :, :], iota_cap.unsqueeze(1).unsqueeze(1).broadcast_to([P, 3, 2, CAP]),
                                  sel_at[:, :, bass.ds(p * 2, 2)].unsqueeze(3).broadcast_to([P, 3, 2, CAP]), ALU.is_equal).then_inc(picked, 1)

            def take_gathered(p):
                for r in range(4):
                    dve.wait_ge(g_mm, p * 4 + (r + 1))
                    dve.tensor_copy(xg[:, 4 * r:4 * r + 4, :], psum[7 - r % 2][:, :].rearrange("p (k s) -> p k s", s=P)).then_inc(g_ev, 1)

            dve.sem_inc(ob_ready, 1)
            dve.sem_inc(g_ev, 2)
            link(dve.tensor_scalar(sel_at[:, :, 0:E], ranked, -FAR, None, ALU.add))
            choose(0)
            take_gathered(0)
            link(dve.tensor_tensor(more, count.unsqueeze(2).broadcast_to([P, E, 4]), b64.unsqueeze(1).broadcast_to([P, E, 4]), ALU.is_gt))
            link(dve.tensor_reduce(nmore, more, AX.X, ALU.add))
            link(dve.tensor_tensor(pair16, ecol.unsqueeze(2).broadcast_to([P, E, E]), ecol.unsqueeze(1).broadcast_to([P, E, E]), ALU.is_gt))
            link(dve.tensor_tensor(pair16, pair16, nmore.unsqueeze(1).broadcast_to([P, E, E]), ALU.mult))
            link(dve.tensor_reduce(cum, pair16, AX.X, ALU.add))
            link(dve.tensor_scalar(bm1, b64, 1.0 / CAP, -1.0, ALU.mult, ALU.add))
            link(dve.tensor_tensor(number, cum.unsqueeze(2).broadcast_to([P, E, 4]), bm1.unsqueeze(1).broadcast_to([P, E, 4]), ALU.add))
            for j in range(NOV):
                link(dve.tensor_scalar(which, number, float(j), None, ALU.is_equal))
                link(dve.tensor_tensor(which, which, more, ALU.mult))
                for tt in range(3):
                    link(dve.tensor_tensor(wtmp, ranked[:, tt, :].unsqueeze(2).broadcast_to([P, E, 4]), b64.unsqueeze(1).broadcast_to([P, E, 4]), ALU.subtract))
                    link(dve.tensor_tensor(wtmp, wtmp, which, ALU.mult))
                    link(dve.tensor_reduce(r1[:, tt, 0:1], wtmp, AX.XY, ALU.add))
                dve.tensor_scalar(sel_at[:, :, E + j:E + j + 1], r1[:, :, 0:1], -FAR, None, ALU.add)
                link(dve.tensor_tensor(wtmp, which, ecol.unsqueeze(2).broadcast_to([P, E, 4]), ALU.mult))
                link(dve.tensor_reduce(planf[:, 1 + j:2 + j], wtmp, AX.XY, ALU.add))
            link(dve.tensor_reduce(planf[:, 0:1], nmore, AX.X, ALU.add))
            link(dve.tensor_scalar(evens, ecol[:, 0:NOVP], 2.0, None, ALU.mult))
            link(dve.tensor_tensor(evens, planf[:, 0:1].broadcast_to([P, NOVP]), evens, ALU.is_gt))
            link(dve.tensor_reduce(planf[:, 0:1], evens, AX.X, ALU.add))
            dve.tensor_copy(plan, planf).then_inc(plan_ready, 1)
            link(dve.tensor_scalar(cum, cum, float(CAP), float(CAP * (E - 1)), ALU.mult, ALU.add))
            link(dve.tensor_tensor(cum, cum, e64, ALU.subtract))
            link(dve.tensor_scalar(rest, rank, float(CAP), None, ALU.is_ge))
            link(dve.tensor_tensor(rest, rest, cum.unsqueeze(1).broadcast_to([P, 3, E]), ALU.mult))
            link(dve.tensor_tensor(rest, rest, rank, ALU.add))
            link(dve.tensor_tensor(rest, rest, e64.unsqueeze(1).broadcast_to([P, 3, E]), ALU.add))
            for w, hot in enumerate((hot1, hot2)):
                link(dve.tensor_tensor(hot, hot, rest, ALU.mult))
                link(dve.tensor_reduce(r1[:, :, w:w + 1], hot, AX.X, ALU.add))
            dve.tensor_copy(rowi, r1[:, :, 0:2]).then_inc(rows_ready, 1)


            def hidden(i, a):
                dve.wait_ge(silu, i * 2 + (a + 1))
                dve.tensor_tensor(hid[a], hid[a], psum[2 * a + 1][:, :], ALU.mult).then_inc(hid_ready, 1)

            def result(i, a):
                dve.wait_ge(w_used, i * UNITS + (C_ALL + 12 * a + 12))
                dve.wait_ge(ob_free, i * 2 + (a + 1))
                dve.tensor_copy(ob[a][:, 0, :], psum[4][:, :])
                dve.tensor_copy(ob[a][:, 1, :], psum[5][:, :]).then_inc(ob_ready, 1)

            def pair(i):
                choose(i + 1)
                hidden(i, 0)
                result(i, 0)
                hidden(i, 1)
                take_gathered(i + 1)
                result(i, 1)

            with dve.Fori(0, NPAIR) as i:
                pair(i)
            dve.wait_ge(plan_ready, 1)
            pairs = dve.value_load(plan[0:1, 0:1], min_val=0, max_val=NOVP)
            with dve.If(pairs > 0):
                with dve.Fori(0, pairs) as j:
                    pair(j + NPAIR)
            dve.wait_ge(ln2_in, 32)
            dve.wait_ge(ax_ready, 3)
            for tt in (2, 0, 1):
                m = P if tt < 2 else NS
                row, second = ring[0:m, 2 * tt, 0:D], ring[0:m, 2 * tt + 1, 0:D]
                dve.wait_ge(r_in[tt][0], 16)
                dve.wait_ge(r_in[tt][1], 16)
                link(dve.scalar_tensor_tensor(out=row, in0=row, scalar=cw[0:m, tt, 0:1], in1=x1[0:m, tt, :], op0=ALU.mult, op1=ALU.add))
                link(dve.scalar_tensor_tensor(out=row, in0=second, scalar=cw[0:m, tt, 1:2], in1=row, op0=ALU.mult, op1=ALU.add))
                for j in range(4):
                    ins = dve.bn_stats(stat[0:m, tt, j, :], row[:, 512 * j:512 * j + 512])
                link(ins)
                dve.bn_aggr(mv[0:m, tt, 0:2], stat[0:m, tt, :, :].rearrange("p n s -> p (n s)")).then_inc(l_var, 1)
                dve.wait_ge(l_std, (2, 0, 1).index(tt) + 2)
                link(dve.reciprocal(mv[0:m, tt, 3:4], mv[0:m, tt, 2:3]))
                normalise(row, tt, m, y_ready)


def kernel(**inputs):
    import numpy as np
    import concourse.bacc as bacc
    from concourse.bass_utils import run_bass_kernel_spmd as run

    a = {k: np.asarray(v) for k, v in inputs.items()}
    f32 = {
        "x_t": np.concatenate([a["x_prompt"][0], a["x_sample"][:, 0]]).T,
        "w_in": a["w_in"][0],
        "ws_t": a["w_s"][0].transpose(2, 0, 1),
        "w00": a["w_s"][0, :, 0, 0],
        "b_s": a["b_s"][0],
        "lng": a["sgu_ln_g"][0], "lnb": a["sgu_ln_b"][0],
        "lbl": a["lb_logits"][0].reshape(H, P).T,
        "normg": a["hgrn_norm_g"][0].reshape(H, P).T,
        "state": a["state_hgrn"][0],
        "woa": a["w_out_a"][0], "wob": a["w_out_b"][0], "wo": a["w_o"][0],
        "ln1g": a["ln1_g"][0], "ln1b": a["ln1_b"][0],
        "rw": a["router_w"], "rb": a["router_b"],
        "wg": a["w_gate"][0], "wu": a["w_up"][0], "wd": a["w_down"][0],
        "ln2g": a["ln2_g"][0], "ln2b": a["ln2_b"][0],
    }
    nc = bacc.Bacc("TRN2", target_bir_lowering=False, num_devices=1)
    arrays, args = {}, []
    for name, v in f32.items():
        arrays[name] = np.ascontiguousarray(v)
        args.append(nc.dram_tensor(name, arrays[name].shape, F32, kind="ExternalInput").ap())
    for name, shape in (("y", (T, D)), ("st_p", (H, P, P)), ("st_s", (NS, H, P, P)), ("v_rows", (NS, W))):
        args.append(nc.dram_tensor(name, shape, F32, kind="ExternalOutput").ap())
    build(nc, *args)
    r = run(nc, [arrays], core_ids=[0]).results[0]
    return (r["y"][:NP_].reshape(1, NP_, D), r["y"][NP_:].reshape(NS, 1, D), r["st_p"].reshape(1, 1, H, P, P),
            r["st_s"].reshape(1, NS, H, P, P), r["v_rows"].reshape(1, NS, 1, W))
```

```python
from contextlib import ExitStack

import numpy as np

import concourse.bass as bass
from concourse import mybir

F32 = mybir.dt.float32
F32R = mybir.dt.float32r
I32 = mybir.dt.int32
ALU = mybir.AluOpType
ACT = mybir.ActivationFunctionType
AX = mybir.AxisListType

P = 128
D = 2048
NP_ = 256
NS = 8
T = NP_ + NS
KD = D // P
H = 8
W = H * P
FF = D // 2
E = 16
EG = 4
G4 = E // EG
CAP = 64
NOV = (2 * T) // CAP
NOVP = NOV // 2
NPAIR = E // 2
NITEM = E + NOV + 2
ALPHA = 2.0 ** 0.25
EPS = 1e-5
SLOT = 4096
FAR = 8192.0

GROUPS = [("f", 24, 8), ("q", 16, 8), ("i", 32, 8), ("v", 8, 8), ("g", 40, 8), ("u", 0, 8), ("ga", 48, 16), ("gb", 64, 16)]
N_IN = 80
N_OUT = 32
Q_OUT = N_OUT // 2
QUANTA = N_IN + Q_OUT + KD
QW = KD * P
UNITS = 24
W_FREE = 8
LEVELS = 8


def start_of(name):
    n = 0
    for g, _, k in GROUPS:
        if g == name:
            return n
        n += k
    raise KeyError(name)


TILE_COL = [first + j for _, first, tiles in GROUPS for j in range(tiles)]


def tiles_done(q):
    return q + 1 if q < N_IN else N_IN + 2 * (q - N_IN + 1) if q < N_IN + Q_OUT else q + 1 + Q_OUT


def build(nc, x_t, w_in, ws_t, w00, b_s, lng, lnb, lbl, normg, state, woa, wob, wo, ln1g, ln1b, rw, rb,
          wg, wu, wd, ln2g, ln2b, y, st_p, st_s, v_s):
    with ExitStack() as ctx:
        def sem(name):
            return ctx.enter_context(nc.semaphore(name))

        scratch = nc.dram_tensor("expert_rows", [(E + NOV) * CAP, D], F32, kind="Internal").ap()

        HT = H * T
        where = [16512]

        def place(name, shape):
            words = int(np.prod(shape[1:]))
            t = nc.alloc_sbuf_tensor_at(name, shape, F32, offset=where[0])
            at_byte = where[0]
            where[0] += (words * 4 + 31) // 32 * 32
            return t, at_byte

        def parts(name, shape, at_byte):
            return nc.alloc_sbuf_tensor_at(name, shape, F32R, offset=at_byte)

        low, low_b = place("ring_low", [P, 4, SLOT])
        low_end, _ = place("low_end", [P, 2 * HT - SLOT])
        high, high_b = place("ring_high", [P, 4, SLOT])
        xt, xt_b = place("xt", [P, KD, T])
        reg_uv, _ = place("reg_uv", [P, 3 * HT])
        reg_pk, pk_b = place("reg_pk", [P, 2 * HT])
        reg_qg, qg_b = place("reg_qg", [P, 2 * HT])

        def ring_slot(s):
            return low[:, s, :] if s < 4 else high[:, s - 4, :]

        raw_w = low[:, 0:2, :].rearrange("p s (h w) -> p (s h) w", w=QW)
        w_lo = parts("w_lo", [P, 4, QW], low_b)
        w_hi01 = parts("w_hi01", [P, 2, QW], low_b + 4 * 4 * QW)
        w_hi2 = parts("w_hi2", [P, QW], high_b + 4 * 13312)
        w_hi = [w_hi01[:, 0, :], w_hi01[:, 1, :], w_hi2[:, :]]

        def hi_of(q):
            return w_hi[q % 3 if q < N_IN + Q_OUT else q % 2]

        x_lo = parts("x_lo", [P, KD, T], low_b + 4 * 3 * SLOT)
        x_hi = parts("x_hi", [P, KD, T], xt_b)
        y_parts = parts("y_parts", [P, 2, 2, H, T], high_b)
        m_hi = parts("m_hi", [P, KD, T], pk_b)
        m_lo = parts("m_lo", [P, KD, T], qg_b)

        def fm(region, at, tiles):
            return region[:, at:at + tiles * T].rearrange("p (k t) -> p k t", t=T)

        vi = fm(reg_uv, 0, H)
        z = reg_uv[:, HT:HT + H * NP_].rearrange("p (k t) -> p k t", t=NP_)
        gb = fm(reg_uv, 0, 2 * H)
        u = fm(reg_uv, 2 * HT, H)
        pcum = fm(reg_pk, 0, H)
        kf = fm(reg_pk, HT, H)
        ga = fm(reg_pk, 0, 2 * H)
        qf = fm(reg_qg, 0, H)
        gf = fm(reg_qg, HT, H)

        raw_x = fm(reg_uv, 0, KD)
        up = high[:, :, :].rearrange("p a b -> p (a b)")
        scum = up[:, 0:2048].rearrange("p (k t) -> p k t", t=NP_)
        sc = up[:, 2048:4096].rearrange("p (h a t) -> p h a t", a=2, t=P)
        scx = up[:, 4096:5120].rearrange("p (h t) -> p h t", t=P)
        itm = up[:, 5120:8192].rearrange("p (a c) -> p a c", c=W)
        vtm = up[:, 8192:11264].rearrange("p (a c) -> p a c", c=W)
        wsm = up[:, 11264:12288].rearrange("p (g t) -> p g t", t=P)
        mask = up[:, 12288:13312].rearrange("p (l t) -> p l t", t=P)
        lngb = reg_uv[:, 2 * HT:2 * HT + 2 * W].rearrange("p (a c) -> p a c", c=W)
        bsb = up[:, 15360:16384].rearrange("p (g t) -> p g t", t=P)
        ktm = reg_uv[:, HT:HT + 2 * W].rearrange("p (a c) -> p a c", c=W)
        s0b = [buf[:, 1024 * a:1024 * (a + 1)].rearrange("p (b v) -> p b v", v=P)
               for buf in (reg_uv[:, HT:HT + 2048], up[:, 0:2048]) for a in range(2)]
        vdb = [reg_uv[0:NS, 1024 * a:1024 * (a + 1)].rearrange("p (b v) -> p b v", v=P) for a in range(2)]

        x1 = reg_uv[:, 3 * HT - 3 * D:3 * HT].rearrange("p (a c) -> p a c", c=D)
        xg = reg_pk[:, 0:KD * P].rearrange("p (k s) -> p k s", s=P)
        ln1p = low[:, 3, :].rearrange("p (a c) -> p a c", c=D)
        ln2p = reg_qg[:, 0:2 * D].rearrange("p (a c) -> p a c", c=D)
        xtf = xt[:, :, :].rearrange("p k t -> p (k t)")
        hid = [xtf[:, 512 * a:512 * (a + 1)] for a in range(2)]
        hidt = [xtf[:, 1024 + 512 * a:1536 + 512 * a].rearrange("p (j f s) -> p j f s", j=4, f=2) for a in range(2)]
        ob = [xtf[:, 2048 + 1024 * a:3072 + 1024 * a].rearrange("p (n c) -> p n c", n=2) for a in range(2)]

        ident, _ = place("ident", [P, P])
        ones, _ = place("ones", [P, P])
        before = reg_qg[:, 2 * D:2 * D + P]
        small, _ = place("small", [P, 608])
        at = [0]

        def take(n):
            a = at[0]
            at[0] += n
            return small[:, a:a + n]

        eps = take(1)
        lbw = take(4 * H).rearrange("p (a h) -> p a h", h=H)
        omlb = take(H)
        ngain = take(H)
        w00b = take(H)
        stat = take(72).rearrange("p (a n s) -> p a n s", a=3, s=6)
        mv = take(3 * 4).rearrange("p (a s) -> p a s", s=4)
        shift = take(1)
        iota_cap = take(CAP)
        iota_i = take(CAP).bitcast(I32)
        back4 = take(EG)
        e64 = take(E)
        ecol = take(E)
        b64 = take(4)
        valid = take(3)
        fqk = take(3 * H * NS).rearrange("p (a h b) -> p a h b", a=3, b=NS)
        sel_at = take(3 * NITEM).rearrange("p (a i) -> p a i", i=NITEM)
        cw = take(6).rearrange("p (a w) -> p a w", w=2)
        rowi = take(6).rearrange("p (a w) -> p a w", w=2).bitcast(I32)
        plan = take(1 + NOV).bitcast(I32)
        pick, _ = place("pick", [P, 3, 2, CAP])
        assert where[0] <= 229368, where

        rt = reg_pk
        rat = [KD * P]

        def rtake(n):
            a = rat[0]
            rat[0] += n
            return rt[:, a:a + n]

        def t3(n=E):
            return rtake(3 * n).rearrange("p (a e) -> p a e", a=3)

        rw_fm, rwb = (up[:, 15360 + KD * E * a:15360 + KD * E * (a + 1)].rearrange("p (k e) -> p k e", e=E) for a in range(2))
        ln1_fm = up[:, 15360 + 2 * KD * E:15360 + 2 * KD * E + 2 * KD].rearrange("p (a k) -> p a k", a=2)
        rwg = pick[:, 0:2, :, :].rearrange("p a b s -> p (a b s)").rearrange("p (k e) -> p k e", e=E)
        neg_gsum, bsum, rbw = (low_end[:, E * a:E * (a + 1)] for a in range(3))
        lg_fm = rtake(T)[0:E, :]
        probs, hot1, hot2, rest, sel, rank, ranked = (t3() for _ in range(7))
        best1, best2, gsum, tmp12 = (rtake(12).unsqueeze(2) for _ in range(4))
        hotg = t3(EG)
        r1 = t3(2)
        count, nmore, cum = (rtake(E) for _ in range(3))
        more, number, which, wtmp = (rtake(4 * E).rearrange("p (e b) -> p e b", b=4) for _ in range(4))
        pair16 = rtake(E * E).rearrange("p (e f) -> p e f", f=E)
        bm1 = rtake(4)
        evens = rtake(NOVP)
        planf = rtake(1 + NOV)
        assert rat[0] <= 2 * HT, rat

        osq = up[:, 2048:2048 + HT].rearrange("p (k t) -> p k t", t=T)
        ostd = up[:, 5120:5120 + HT].rearrange("p (k t) -> p k t", t=T)
        ks_rows = up[:, 12288:13312]

        def halves(buf, h, side):
            return buf[:, :, 0:NP_].rearrange("p k (b w x) -> p k b w x", w=2, x=h)[:, :, :, side, :]

        def total(buf, h, side):
            return halves(buf, h, side)[:, :, :, h - 1:h].broadcast_to([P, H, NP_ // (2 * h), h])

        psum = [ctx.enter_context(nc.psum_tensor(f"bank{b}", [P, 512], F32)) for b in range(8)]

        x_in = [sem(f"x_in{q}") for q in range(4)]; side_in = sem("side_in"); ln1_in = sem("ln1_in"); router_in = sem("router_in")
        landed = [sem(f"landed{s}") for s in range(8)]
        w_used = sem("w_used")
        raw_in = [sem(f"raw_in{s}") for s in range(4)]; hi_ready = sem("hi_ready"); lo_ready = sem("lo_ready")
        xh_ready = sem("xh_ready"); xl_ready = sem("xl_ready"); yh_ready = sem("yh_ready"); yl_ready = sem("yl_ready")
        m_sum = sem("m_sum"); mh_ready = sem("mh_ready"); ml_ready = sem("ml_ready"); x_again_in = sem("x_again_in")
        consts = sem("consts"); pool_chain = sem("pool_chain")
        gemm = sem("gemm"); act_evac = sem("act_evac"); dve_evac = sem("dve_evac")
        lb_exp = sem("lb_exp"); lb_sub = sem("lb_sub")
        f_ready = sem("f_ready"); logf = sem("logf"); k_ready = sem("k_ready")
        i_tr = sem("i_tr"); i_ev = sem("i_ev"); v_tr = sem("v_tr"); v_ev = sem("v_ev")
        lvl_exp = sem("lvl_exp"); lvl_z = sem("lvl_z"); lvl_mm = sem("lvl_mm"); lvl_cp = sem("lvl_cp"); lvl_up = sem("lvl_up")
        kf_tr = sem("kf_tr"); kf_ev = sem("kf_ev"); st_mm = sem("st_mm"); st_ev = sem("st_ev")
        ks_tr = sem("ks_tr"); ks_ev = sem("ks_ev"); s0_in = [sem(f"s0_in{a}") for a in range(4)]
        s_vd = sem("s_vd"); s_mm = sem("s_mm"); s_new = sem("s_new"); s_o = sem("s_o"); s_out = [sem(f"s_out{a}") for a in range(4)]
        o_mm = sem("o_mm"); o_ev = sem("o_ev"); vs_tr = sem("vs_tr"); sgu_mm = sem("sgu_mm"); sgu_ev = sem("sgu_ev")
        v_ln = sem("v_ln"); v_ln_var = sem("v_ln_var"); v_std = sem("v_std")
        o_sq = sem("o_sq"); n_mm = sem("n_mm"); n_std = sem("n_std"); yb_ready = sem("yb_ready")
        upper_free = sem("upper_free"); outs = sem("outs"); vs_out = sem("vs_out")
        h_tr = sem("h_tr"); h_ev = sem("h_ev"); l_var = sem("l_var"); l_std = sem("l_std"); l_inv = sem("l_inv"); l_shift = sem("l_shift"); x1s_norm = sem("x1s_norm"); x1s_ready = sem("x1s_ready"); x1_ready = sem("x1_ready")
        rw_ready = sem("rw_ready"); sums_mm = sem("sums_mm"); sums_ready = sem("sums_ready"); raw_mm = sem("raw_mm"); raw_ev = sem("raw_ev"); lg_mm = sem("lg_mm"); r_max = sem("r_max"); r_exp = sem("r_exp")
        sel_ready = sem("sel_ready"); rank_mm = sem("rank_mm"); plan_ready = sem("plan_ready"); rows_ready = sem("rows_ready")
        picked = sem("picked"); g_mm = sem("g_mm"); g_ev = sem("g_ev")
        silu = sem("silu"); hid_ready = sem("hid_ready"); hid_tr = sem("hid_tr"); hid_ev = sem("hid_ev")
        ob_ready = sem("ob_ready"); ob_free = sem("ob_free"); ob_out = [sem("ob_out0"), sem("ob_out1")]
        ln2_in = sem("ln2_in"); ax_ready = sem("ax_ready"); r_in = [[sem(f"r_in{t}{w}") for w in range(2)] for t in range(3)]; y_ready = sem("y_ready"); ys_ready = sem("ys_ready"); y_out = sem("y_out")
        s_weighted = sem("s_weighted"); s_sum = sem("s_sum"); s_shift = sem("s_shift"); s_norm = sem("s_norm"); zeroed = sem("zeroed"); zero_out = sem("zero_out"); dve_chain = sem("dve_chain")

        I0, V0, U0, GA0, GB0 = (start_of(s) for s in ("i", "v", "u", "ga", "gb"))
        DIAG_AT, I_TR_AT, V_TR_AT = I0 + 1, (I0 + 5, V0), (V0 + 4, V0 + 8)
        LEVEL_AT = [I0 + 4, V0 + 1, V0 + 5, V0 + 10, V0 + 15, V0 + 18, V0 + 21, V0 + 24]
        KFIN_AT, STATE_AT = GA0 + 2, GA0 + 4
        SAMPLE_AT = STATE_AT + 1
        O_AT = SAMPLE_AT + H + 1
        SGU_AT = O_AT + 4
        NORM_AT = SGU_AT + 4
        SUMS_AT = 8
        Y_AT = NORM_AT + 6
        block = ctx.enter_context(nc.Block())

        @block.sync
        def _(sp):
            def load_x(q):
                sp.dma_start(raw_x[:, 4 * q:4 * q + 4, :], x_t[4 * P * q:4 * P * (q + 1), :].rearrange("(k p) t -> p k t", p=P)).then_inc(x_in[q], 16)

            load_x(0)
            for q in range(QUANTA):
                if q >= 4:
                    sp.wait_ge(gemm, tiles_done(q - 4))
                if q < N_IN:
                    col = TILE_COL[q] * P
                    src, kk = w_in[:, col:col + P], KD
                elif q < N_IN + Q_OUT:
                    j = (q - N_IN) // 2
                    src, kk = (woa, wob)[(q - N_IN) % 2][:, 2 * P * j:2 * P * (j + 1)], H
                else:
                    j = q - N_IN - Q_OUT
                    src, kk = wo[:, P * j:P * (j + 1)], KD
                sp.dma_start(raw_w[:, q % 4, :].rearrange("p (k n) -> p k n", k=kk),
                             src.rearrange("(k p) n -> p k n", p=P)).then_inc(raw_in[q % 4], 16)
                if q == 0:
                    for x in range(1, 4):
                        load_x(x)
                if q == N_IN + 8:
                    sp.dma_start(xt[:, :, :], x_t.rearrange("(k p) t -> p k t", p=P)).then_inc(x_again_in, 16)

            def expert_pair(i, experts):
                for a in range(2):
                    for part, wt in enumerate((wg, wu, wd)):
                        for q in range(4):
                            m = 12 * a + 4 * part + q
                            s = (m + 4) % 8
                            sp.wait_ge(w_used, i * UNITS + (W_FREE + m - 7))
                            rows = (FF if part == 2 else D) // 4
                            src = wt[experts[a], q * rows:(q + 1) * rows, :].rearrange("(k p) n -> p k n", p=P)
                            sp.dma_start(ring_slot(s).rearrange("p (k n) -> p k n", k=rows // P), src).then_inc(landed[s], 16)

            with sp.Fori(0, NPAIR) as i:
                expert_pair(i, (i * 2, i * 2 + 1))
            sp.wait_ge(plan_ready, 1)
            pairs = sp.value_load(plan[0:1, 0:1], min_val=0, max_val=NOVP)
            with sp.If(pairs > 0):
                with sp.Fori(0, pairs) as j:
                    e0 = sp.value_load(plan[0:1, bass.ds(j * 2 + 1, 1)], min_val=0, max_val=E - 1)
                    e1 = sp.value_load(plan[0:1, bass.ds(j * 2 + 2, 1)], min_val=0, max_val=E - 1)
                    expert_pair(j + NPAIR, (e0, e1))
            sp.nop()
            for tt, ready, n, cols in ((0, y_ready, 1, slice(0, D)), (2, ys_ready, 1, slice(0, D)),
                                       (1, y_ready, 2, slice(0, D // 2)), (1, y_ready, 3, slice(D // 2, D))):
                m = P if tt < 2 else NS
                sp.wait_ge(ready, n)
                sp.dma_start(y[P * tt:P * tt + m, cols], ring_slot(2 * tt)[0:m, cols]).then_inc(y_out, 16)
            sp.wait_ge(y_out, 16 * 4)

        @block.gpsimd
        def _(pool):
            n = [0]

            def link(ins):
                n[0] += 1
                ins.then_inc(pool_chain, 1)
                pool.wait_ge(pool_chain, n[0])

            with nc.allow_non_contiguous_dma("small parameters"):
                pool.dma_start(lbw[:, 0, :], lbl).then_inc(side_in, 16)
                pool.dma_start(ngain, normg).then_inc(side_in, 16)
                pool.dma_start(w00b, w00.partition_broadcast(P)).then_inc(side_in, 16)
                pool.dma_start(wsm, ws_t).then_inc(side_in, 16)
                pool.dma_start(bsb, b_s.partition_broadcast(P)).then_inc(side_in, 16)
                pool.dma_start(lngb[:, 0, :], lng.partition_broadcast(P)).then_inc(side_in, 16)
                pool.dma_start(lngb[:, 1, :], lnb.partition_broadcast(P)).then_inc(side_in, 16)
            link(pool.memset(ident[:, :], 0.0))
            link(pool.affine_select(out=ident[:, :], in_=ident[:, :], compare_op=ALU.not_equal, fill=1.0, base=0,
                                    pattern=[[-1, P]], channel_multiplier=1))
            pool.memset(ones[:, :], 1.0)
            pool.memset(eps, EPS)
            link(pool.memset(mask[:, :, :], 0.0))
            pool.affine_select(out=mask[:, 0, :], in_=mask[:, 0, :], compare_op=ALU.not_equal, fill=1.0, base=0,
                               pattern=[[-1, P]], channel_multiplier=1)
            for lv in range(7):
                h = 1 << lv
                pool.affine_select(out=mask[:, 1 + lv, :], in_=mask[:, 1 + lv, :], compare_op=ALU.is_ge, fill=1.0, base=0,
                                   pattern=[[-h, P // h], [0, h]], channel_multiplier=1)
            link(pool.memset(valid, 1.0))
            link(pool.affine_select(out=valid[:, 2:3], in_=valid[:, 2:3], compare_op=ALU.is_ge, fill=0.0, base=NS - 1,
                                    pattern=[[0, 1]], channel_multiplier=-1))
            for out, base, step, k in ((iota_cap, 0, 1, CAP), (back4, -EG, 1, EG), (e64, 0, CAP, E), (ecol, 0, 1, E), (b64, CAP, CAP, 4)):
                link(pool.iota(iota_i[:, 0:k], pattern=[[step, k]], base=base, channel_multiplier=0))
                link(pool.tensor_copy(out, iota_i[:, 0:k]))
            pool.wait_ge(side_in, 16 * 7)
            link(pool.affine_select(out=wsm, in_=wsm, compare_op=ALU.is_ge, fill=0.0, base=0,
                                    pattern=[[0, H], [1, P]], channel_multiplier=-1))
            pool.nop().then_inc(consts, 1)
            pool.wait_ge(zeroed, 1)
            pool.wait_ge(gemm, 6)
            for a in range(2):
                pool.dma_start(scratch[CAP * (E + 4 * a):CAP * (E + 4 * a + 4), :].rearrange("(p r) c -> p (r c)", p=P),
                               up[:, 0:4096]).then_inc(zero_out, 16)
            pool.wait_ge(st_ev, 1)
            pool.dma_start(st_p.rearrange("h k v -> k h v"), scum[:, :, 0:P]).then_inc(outs, 16)
            def load_state(h):
                pool.dma_start(s0b[h % 4], state[:, h].rearrange("b k v -> k b v")).then_inc(s0_in[h % 4], 16)

            for h in range(H):
                a = h % 4
                if h == 0:
                    pool.wait_ge(st_mm, 1)
                    for b in range(2):
                        load_state(b)
                    pool.wait_ge(outs, 16)
                    for b in range(2, 4):
                        load_state(b)
                pool.wait_ge(s_new, h + 1)
                pool.wait_ge(s_o, h + 1)
                pool.dma_start(st_s[:, h].rearrange("b k v -> k b v"), s0b[a]).then_inc(s_out[a], 16)
                if h == 4:
                    pool.wait_ge(v_ln, 3)
                    pool.dma_start(v_s, vtm[0:NS, 2, :]).then_inc(vs_out, 16)
                if 1 <= h and h + 3 < H:
                    pool.wait_ge(s_out[(h - 1) % 4], 16)
                    load_state(h + 3)
            pool.wait_ge(gemm, N_IN)
            pool.dma_start(rbw, rb.partition_broadcast(P)).then_inc(router_in, 16)
            pool.wait_ge(upper_free, 1)
            pool.dma_start(rw_fm, rw.rearrange("(k p) e -> p k e", p=P)).then_inc(router_in, 16)
            with nc.allow_non_contiguous_dma("small parameters"):
                pool.dma_start(ln1_fm[:, 0, :], ln1g.rearrange("(k p) -> p k", p=P)).then_inc(router_in, 16)
                pool.dma_start(ln1_fm[:, 1, :], ln1b.rearrange("(k p) -> p k", p=P)).then_inc(router_in, 16)
            for a, par in enumerate((ln1g, ln1b)):
                pool.wait_ge(gemm, N_IN + N_OUT // 2 + 8 * a)
                pool.dma_start(ln1p[:, a, :], par.partition_broadcast(P)).then_inc(ln1_in, 16)
            pool.wait_ge(gemm, N_IN + N_OUT + KD)
            link(pool.memset(before, 1.0))
            pool.affine_select(out=before, in_=before, compare_op=ALU.is_ge, fill=0.0, base=-1,
                               pattern=[[1, P]], channel_multiplier=-1).then_inc(consts, 1)
            pool.wait_ge(x1s_norm, 1)
            pool.wait_ge(ln1_in, 32)
            row = x1[0:NS, 2, :]
            link(pool.tensor_tensor(row, row, ln1p[0:NS, 0, :], ALU.mult))
            pool.tensor_tensor(row, row, ln1p[0:NS, 1, :], ALU.add).then_inc(x1s_ready, 1)
            pool.dma_start(ln2p[:, 0, :], ln2g.partition_broadcast(P)).then_inc(ln2_in, 16)
            pool.dma_start(ln2p[:, 1, :], ln2b.partition_broadcast(P)).then_inc(ln2_in, 16)
            pool.sem_inc(ob_free, 2)

            def store_pair(i, rows):
                for a in range(2):
                    pool.wait_ge(ob_ready, i * 2 + (a + 2))
                    for half in range(2):
                        dst = scratch[bass.ds(rows + CAP * a, CAP), :].rearrange("s (n f c) -> f s n c", n=2, f=2)[half]
                        pool.dma_start(dst, ob[a][64 * half:64 * half + 64, :, :]).then_inc(ob_out[a], 16)
                    pool.wait_ge(ob_out[a], i * 32 + 32)
                    pool.sem_inc(ob_free, 1)

            with pool.Fori(0, NPAIR) as i:
                store_pair(i, i * (2 * CAP))
            pool.wait_ge(plan_ready, 1)
            pairs = pool.value_load(plan[0:1, 0:1], min_val=0, max_val=NOVP)
            with pool.If(pairs > 0):
                with pool.Fori(0, pairs) as j:
                    store_pair(j + NPAIR, (j + NPAIR) * (2 * CAP))
            pool.wait_ge(rows_ready, 1)
            pool.wait_ge(ob_free, 2 + E)
            for tt in (0, 2, 1):
                m = P if tt < 2 else NS
                for w in range(2):
                    pool.indirect_dma_start(out=ring_slot(2 * tt + w)[0:m, 0:D], out_offset=None, in_=scratch[:, :],
                                            in_offset=bass.IndirectOffsetOnAxis(ap=rowi[0:m, tt, w:w + 1], axis=0)).then_inc(r_in[tt][w], 16)
            row, second = ring_slot(4)[0:NS, 0:D], ring_slot(5)[0:NS, 0:D]
            pool.wait_ge(s_weighted, 1)
            link(pool.tensor_tensor(row, row, x1[0:NS, 2, :], ALU.add))
            pool.wait_ge(s_weighted, 2)
            pool.tensor_tensor(row, row, second, ALU.add).then_inc(s_sum, 1)
            pool.wait_ge(s_norm, 1)
            link(pool.tensor_tensor(row, row, ln2p[0:NS, 0, :], ALU.mult))
            pool.tensor_tensor(row, row, ln2p[0:NS, 1, :], ALU.add).then_inc(ys_ready, 1)
            pool.wait_ge(outs, 16)
            pool.wait_ge(vs_out, 16)
            for a in range(4):
                pool.wait_ge(s_out[a], 16 * 2)

        @block.tensor
        def _(pe):
            def gemm_tile(n, hi, lo, of_hi, of_lo):
                if n >= 4:
                    p = n - 4
                    if p < N_IN:
                        pe.wait_ge(act_evac, p + 1)
                    else:
                        pe.wait_ge(dve_evac, p - N_IN + 1)
                kk = len(hi)
                for k in range(kk):
                    if n == 0 and k % 4 == 0:
                        pe.wait_ge(xl_ready, k // 4 + 1)
                    if n == N_IN + N_OUT and k % 2 == 0:
                        pe.wait_ge(ml_ready, k // 2 + 1)
                    out = psum[n % 4][:, 0:T]
                    pe.matmul(out, hi[k], of_hi[:, k, :], start=(k == 0), stop=False)
                    pe.matmul(out, hi[k], of_lo[:, k, :], start=False, stop=False)
                    mm = pe.matmul(out, lo[k], of_hi[:, k, :], start=False, stop=(k == kk - 1))
                mm.then_inc(gemm, 1)

            def transposes(done, src, batch, evacuated):
                if batch:
                    pe.wait_ge(evacuated, 3)
                for tt in range(3):
                    m = P if tt < 2 else NS
                    for j in range(4):
                        mm = pe.transpose(psum[4 + tt][0:m, P * j:P * (j + 1)], src[:, 4 * batch + j, P * tt:P * tt + m], ident[:, :])
                    mm.then_inc(done, 1)

            def level(lv):
                if lv < 0:
                    a, b = kf, qf
                    pe.wait_ge(consts, 1)
                    pe.wait_ge(k_ready, 1)
                else:
                    a, b = z, z
                    pe.wait_ge(lvl_z, lv + 1)
                if lv == 7:
                    for h in range(H):
                        if h % 4 == 0:
                            pe.wait_ge(lvl_cp, 4 * 7 + h // 4 + 1)
                        mm = pe.matmul(psum[4 + h // 4][:, P * (h % 4):P * (h % 4 + 1)], z[:, h, 0:P], z[:, h, P:2 * P], start=True, stop=True)
                        if h % 4 == 3:
                            mm.then_inc(lvl_mm, 1)
                    return
                for r in range(4):
                    if lv == 1 and r < 3:
                        pe.wait_ge(i_ev, 6)
                    if lv == 2 and r < 3:
                        pe.wait_ge(v_ev, 3)
                    if lv == 3 and r < 3:
                        pe.wait_ge(v_ev, 6)
                    if lv >= 0:
                        pe.wait_ge(lvl_cp, 4 * lv + r + 1)
                    for j in range(4):
                        h, tt = 2 * r + j // 2, j % 2
                        mm = pe.matmul(psum[4 + r][:, P * j:P * (j + 1)], a[:, h, P * tt:P * tt + P], b[:, h, P * tt:P * tt + P], start=True, stop=True)
                    mm.then_inc(lvl_mm, 1)

            def v_transposes(batch):
                pe.wait_ge(act_evac, V0 + 4 * batch + 4)
                pe.wait_ge(lvl_cp, 4 * (3 if batch == 0 else 4))
                for tt in range(3):
                    m = P if tt < 2 else NS
                    for j in range(4):
                        mm = pe.transpose(psum[4 + tt][0:m, P * j:P * (j + 1)], vi[:, 4 * batch + j, P * tt:P * tt + m], ident[:, :])
                    mm.then_inc(v_tr, 1)

            def side(n):
                if n == I_TR_AT[0]:
                    pe.wait_ge(lvl_cp, 8)
                    pe.wait_ge(act_evac, I0 + 4)
                    transposes(i_tr, vi, 0, i_ev)
                if n == I_TR_AT[1]:
                    pe.wait_ge(act_evac, I0 + 8)
                    transposes(i_tr, vi, 1, i_ev)
                if n == DIAG_AT:
                    level(-1)
                if n in LEVEL_AT:
                    level(LEVEL_AT.index(n))
                if n in V_TR_AT:
                    v_transposes(V_TR_AT.index(n))
                if n == KFIN_AT:
                    pe.wait_ge(kf_ev, 1)
                    for r in range(4):
                        if r < 2:
                            pe.wait_ge(lvl_cp, 4 * 8 + r + 1)
                        for j in range(4):
                            mm = pe.transpose(psum[4 + r][:, P * j:P * (j + 1)], z[:, 4 * (r % 2) + j, P * (r // 2):P * (r // 2) + P], ident[:, :])
                        mm.then_inc(kf_tr, 1)
                if n == STATE_AT:
                    for r in range(2):
                        pe.wait_ge(kf_ev, 5)
                        for j in range(4):
                            h = 4 * r + j
                            for tt in range(2):
                                mm = pe.matmul(psum[4 + r][:, P * j:P * (j + 1)], ktm[:, tt, P * h:P * h + P], itm[:, tt, P * h:P * h + P],
                                               start=(tt == 0), stop=(tt == 1))
                    mm.then_inc(st_mm, 1)
                    for r in range(2):
                        for j in range(4):
                            mm = pe.transpose(psum[6 + r][0:NS, P * j:P * (j + 1)], fqk[:, 2, 4 * r + j, :], ident[:, :])
                    mm.then_inc(ks_tr, 1)
                if SAMPLE_AT <= n < SAMPLE_AT + H:
                    h = n - SAMPLE_AT
                    pe.wait_ge(ks_ev, 1)
                    pe.wait_ge(st_ev, 1)
                    pe.wait_ge(s_vd, h + 1)
                    for r in range(2):
                        if h:
                            pe.wait_ge(s_new, h)
                        mm = pe.matmul(psum[4 + r][:, :], ks_rows[0:NS, P * h:P * h + P], vdb[h % 2][:, 4 * r:4 * r + 4, :], start=True, stop=True)
                    mm.then_inc(s_mm, 1)
                    if h:
                        sample_out(h - 1)
                if n == SAMPLE_AT + H:
                    sample_out(7)
                if O_AT <= n < O_AT + 4:
                    for h in (2 * (n - O_AT), 2 * (n - O_AT) + 1):
                        b = psum[(4, 5, 7)[h % 3]]
                        if h >= 3:
                            pe.wait_ge(o_ev, h - 2)
                        else:
                            pe.wait_ge(s_new, 8)
                            pe.wait_ge(ks_ev, 1)
                        pe.matmul(b[:, 0:P], itm[:, 0, P * h:P * h + P], sc[:, h, 0, :], start=True, stop=True)
                        pe.matmul(b[:, P:2 * P], itm[:, 0, P * h:P * h + P], scx[:, h, :], start=True, stop=False)
                        pe.matmul(b[:, P:2 * P], itm[:, 1, P * h:P * h + P], sc[:, h, 1, :], start=False, stop=True).then_inc(o_mm, 1)
                if n == SGU_AT:
                    pe.wait_ge(v_ln, 3)
                    pe.wait_ge(o_ev, 9)
                    for g in range(H):
                        mm = pe.transpose(psum[6][:, NS * g:NS * (g + 1)], vtm[0:NS, 2, P * g:P * g + P], ident[0:NS, 0:NS])
                    mm.then_inc(vs_tr, 1)
                if SGU_AT <= n < SGU_AT + 4:
                    for g in (2 * (n - SGU_AT), 2 * (n - SGU_AT) + 1):
                        b = psum[(4, 5, 7)[g % 3]]
                        if g >= 3:
                            pe.wait_ge(sgu_ev, g - 2)
                        else:
                            pe.wait_ge(o_ev, 9)
                        for tt in range(2):
                            mm = pe.matmul(b[:, P * tt:P * tt + P], vtm[:, tt, P * g:P * g + P], wsm[:, g, :], start=True, stop=True)
                        mm.then_inc(sgu_mm, 1)
                if n == NORM_AT:
                    for h in range(H):
                        b = psum[4 + h % 4]
                        if h >= 4:
                            pe.wait_ge(n_std, h - 3)
                        else:
                            pe.wait_ge(sgu_ev, 9)
                            pe.wait_ge(o_sq, 1)
                        pe.matmul(b[:, 0:T], ones[:, :], osq[:, h, :], start=True, stop=True).then_inc(n_mm, 1)

            def sample_out(h):
                pe.wait_ge(s_new, h + 1)
                for b in range(NS):
                    mm = pe.matmul(psum[6][:, NS * h + b:NS * h + b + 1], s0b[h % 4][:, b, :], fqk[:, 1, h, b:b + 1], start=True, stop=True)
                mm.then_inc(s_o, 1)

            def split_of(q, kk):
                pe.wait_ge(lo_ready, q + 1)
                return tuple(w.rearrange("p (k n) -> p k n", k=kk) for w in (hi_of(q), w_lo[:, q % 4, :]))

            for n in range(N_IN):
                hi, lo = split_of(n, KD)
                gemm_tile(n, [hi[:, k, :] for k in range(KD)], [lo[:, k, :] for k in range(KD)], x_hi, x_lo)
                side(n)
            for r in range(Q_OUT):
                br = r % 2
                hi, lo = split_of(N_IN + r, H)
                if r < 2:
                    pe.wait_ge(yl_ready, r + 1)
                for f in range(2):
                    cols = slice(P * f, P * f + P)
                    gemm_tile(N_IN + 2 * r + f, [hi[:, k, cols] for k in range(H)], [lo[:, k, cols] for k in range(H)],
                              y_parts[:, br, 0, :, :], y_parts[:, br, 1, :, :])
                if r == SUMS_AT:
                    pe.wait_ge(rw_ready, 1)
                    for a, w in enumerate((rwg, rwb)):
                        mm = pe.matmul(psum[7][:, KD * E * a:KD * E * (a + 1)], ones[:, :], w.rearrange("p k e -> p (k e)"), start=True, stop=True)
                    mm.then_inc(sums_mm, 1)

            def raw_logits(k):
                pe.wait_ge(dve_evac, N_OUT + k + 1)
                if k == 0:
                    pe.wait_ge(sums_ready, 1)
                return pe.matmul(psum[7][0:E, 0:T], rwg[:, k, :], xt[:, k, :], start=(k == 0), stop=(k == KD - 1))

            def to_tm(batch):
                pe.wait_ge(dve_evac, N_OUT + 4 * batch + 4)
                for tt in range(3):
                    m = P if tt < 2 else NS
                    if batch:
                        pe.wait_ge(h_ev, 3 * (batch - 1) + tt + 1)
                    for j in range(4):
                        mm = pe.transpose(psum[4 + tt][0:m, P * j:P * (j + 1)], xt[:, 4 * batch + j, P * tt:P * tt + m], ident[:, :])
                    mm.then_inc(h_tr, 1)

            for j in range(KD):
                n = N_IN + N_OUT + j
                hi, lo = split_of(N_IN + Q_OUT + j, KD)
                gemm_tile(n, [hi[:, k, :] for k in range(KD)], [lo[:, k, :] for k in range(KD)], m_hi, m_lo)
                if j == 0:
                    pe.wait_ge(gemm, N_IN + N_OUT)
                    pe.sem_inc(w_used, 4)
                if j:
                    raw_logits(j - 1)
                if j % 4 == 1 and j > 4:
                    to_tm(j // 4 - 1)
            to_tm(3)
            raw_logits(KD - 1).then_inc(raw_mm, 1)
            pe.wait_ge(raw_ev, 1)
            pe.sem_inc(w_used, 3)
            for tt in range(3):
                m = P if tt < 2 else NS
                mm = pe.transpose(psum[0][0:m, E * tt:E * (tt + 1)], lg_fm[:, P * tt:P * tt + m], ident[0:E, 0:E])
            mm.then_inc(lg_mm, 1)
            pe.wait_ge(sel_ready, 1)
            pe.wait_ge(consts, 2)
            pe.matmul(psum[5][:, 0:3 * E], before[:, :], sel.rearrange("p a e -> p (a e)"), start=True, stop=False)
            for s in range(2):
                pe.matmul(psum[5][:, E * (s + 1):3 * E].rearrange("p (a e) -> p a e", e=E), ones[:, :],
                          sel[:, s:s + 1, :].broadcast_to([P, 2 - s, E]), start=False, stop=(s == 1))
            for s in range(3):
                mm = pe.matmul(psum[6][:, 0:E], ones[:, :], sel[:, s, :], start=(s == 0), stop=(s == 2))
            mm.then_inc(rank_mm, 1)

            def gather_part(p, r):
                b = psum[7 - r % 2]
                pe.wait_ge(g_ev, p * 4 + (r + 1))
                for j in range(4):
                    for tt in range(3):
                        k = 4 * r + j
                        mm = pe.matmul(b[:, P * j:P * (j + 1)], x1[:, tt, P * k:P * k + P],
                                       pick[:, tt, :, :].rearrange("p a s -> p (a s)"), start=(tt == 0), stop=(tt == 2))
                mm.then_inc(g_mm, 1)

            def gather(p):
                pe.wait_ge(picked, p + 1)
                for r in range(4):
                    gather_part(p, r)

            def unit(i, m):
                pe.wait_ge(landed[(m + 4) % 8], i * 48 + 16 * (m // 8 + 1))
                return ring_slot((m + 4) % 8)

            def gate_or_up(i, a, part, q):
                wt = unit(i, 12 * a + 4 * part + q).rearrange("p (k n) -> p k n", k=4)
                for kk in range(4):
                    k = 4 * q + kk
                    for half in range(2):
                        mm = pe.matmul(psum[2 * a + part][64 * half:64 * half + 64, :], xg[:, k, CAP * a:CAP * a + CAP],
                                       wt[:, kk, 512 * half:512 * half + 512], start=(k == 0), stop=(k == KD - 1))
                mm.then_inc(w_used, 1)

            def expert(i, a, gathered=True):
                if gathered and a == 0:
                    pe.wait_ge(g_ev, i * 4 + 6)
                for part in range(2):
                    for q in range(4):
                        if not gathered and part == 0:
                            pe.wait_ge(x1_ready, 2 + q // 2)
                            gather_part(0, q)
                            if q == 0:
                                pe.wait_ge(x1_ready, 3)
                                pe.sem_inc(w_used, 1)
                            pe.wait_ge(g_ev, 3 + q)
                        gate_or_up(i, a, part, q)

            def down(i, a):
                pe.wait_ge(hid_ready, i * 2 + (a + 1))
                if a:
                    pe.wait_ge(g_ev, i * 4 + 10)
                for j in range(4):
                    mm = pe.transpose(psum[6][:, P * j:P * (j + 1)], hid[a][:, P * j:P * (j + 1)], ident[:, :])
                mm.then_inc(hid_tr, 1)
                pe.wait_ge(hid_ev, i * 2 + (a + 1))
                pe.wait_ge(ob_ready, i * 2 + (a + 1))
                for q in range(4):
                    wt = unit(i, 12 * a + 8 + q).rearrange("p (k n) -> p k n", k=2)
                    for kk in range(2):
                        k = 2 * q + kk
                        for nn in range(4):
                            mm = pe.matmul(psum[4 + nn // 2][64 * (nn % 2):64 * (nn % 2) + 64, :], hidt[a][:, k % 4, k // 4, :],
                                           wt[:, kk, 512 * nn:512 * nn + 512], start=(k == 0), stop=(k == 7))
                    mm.then_inc(w_used, 1)

            def pair(i, gathered=True):
                expert(i, 0, gathered)
                down(i, 0)
                expert(i, 1)
                gather(i + 1)
                down(i, 1)

            pe.wait_ge(x1s_ready, 1)
            pe.wait_ge(picked, 1)
            pair(0, gathered=False)
            with pe.Fori(1, NPAIR) as i:
                pair(i)
            pe.wait_ge(plan_ready, 1)
            pairs = pe.value_load(plan[0:1, 0:1], min_val=0, max_val=NOVP)
            with pe.If(pairs > 0):
                with pe.Fori(0, pairs) as j:
                    pair(j + NPAIR)
            pe.nop()

        @block.scalar
        def _(act):
            evac_of = {}
            n = 0
            for name, _, tiles in GROUPS:
                for j in range(tiles):
                    evac_of[n] = (name, j)
                    n += 1

            def hi_part(q):
                if q < QUANTA:
                    if q >= 3:
                        ahead = 3 if q < N_IN + Q_OUT + 2 else 2
                        act.wait_ge(gemm, tiles_done(q - ahead))
                    act.wait_ge(raw_in[q % 4], 16 * (q // 4 + 1))
                    act.copy(hi_of(q), raw_w[:, q % 4, :]).then_inc(hi_ready, 1)

            hi_part(0)
            for x in range(4):
                act.wait_ge(x_in[x], 16)
                act.copy(x_hi[:, 4 * x:4 * x + 4, :], raw_x[:, 4 * x:4 * x + 4, :]).then_inc(xh_ready, 1)
            hi_part(1)
            hi_part(2)
            def exps(lv):
                if lv:
                    act.wait_ge(lvl_mm, 4 * (lv + 1))
                    act.wait_ge(lvl_up, lv)
                else:
                    act.wait_ge(logf, 1)
                    act.wait_ge(zeroed, 1)
                h = 1 << lv
                act.activation(halves(z, h, 1), halves(pcum, h, 1), ACT.Exp).then_inc(lvl_exp, 1)
                act.activation(halves(z, h, 0), halves(scum, h, 0), ACT.Exp).then_inc(lvl_exp, 1)

            func = {"q": ACT.Silu, "i": ACT.Copy, "v": ACT.Gelu_apprx_tanh, "u": ACT.Gelu_apprx_tanh, "g": ACT.Silu,
                    "ga": ACT.Sigmoid, "gb": ACT.Sigmoid}
            dest = {"q": qf, "i": vi, "v": vi, "u": u, "g": gf, "ga": ga, "gb": gb}
            for n in range(N_IN):
                name, j = evac_of[n]
                act.wait_ge(gemm, n + 1)
                src = psum[n % 4][:, 0:T]
                if name == "f":
                    act.activation(pcum[:, j, :], src, ACT.Sigmoid)
                    act.activation(kf[:, j, :], src, ACT.Sigmoid, scale=-1.0).then_inc(act_evac, 1)
                else:
                    if name == "v" and j == 0:
                        act.wait_ge(i_tr, 6)
                    if name == "u" and j == 0:
                        act.wait_ge(v_ln, 3)
                    if name == "ga" and j == 0:
                        act.wait_ge(lvl_up, 8)
                    if name == "ga" and j == 8:
                        act.wait_ge(kf_ev, 1)
                    if name == "gb" and j == 0:
                        act.wait_ge(s_o, 8)
                        act.wait_ge(s_out[0], 32)
                        act.wait_ge(s_out[1], 32)
                    act.activation(dest[name][:, j, :], src, func[name]).then_inc(act_evac, 1)
                hi_part(n + 3)
                if n == 1:
                    act.wait_ge(consts, 1)
                    act.wait_ge(lb_sub, 1)
                    act.activation(lbw[:, 1, :], lbw[:, 1, :], ACT.Exp).then_inc(lb_exp, 1)
                if name == "q" and j == 3:
                    act.wait_ge(f_ready, 1)
                    act.activation(pcum[:, :, 0:NP_], pcum[:, :, 0:NP_], ACT.Ln).then_inc(logf, 1)
                if n == DIAG_AT:
                    exps(0)
                if n in LEVEL_AT[:-1]:
                    exps(LEVEL_AT.index(n) + 1)
                if n == LEVEL_AT[-1]:
                    act.wait_ge(lvl_mm, 34)
                    act.wait_ge(lvl_up, 8)
                    act.activation(z, scum, ACT.Exp).then_inc(lvl_exp, 1)
                if n == LEVEL_AT[3] + 1:
                    for tt in range(3):
                        m = P if tt < 2 else NS
                        act.wait_ge(v_ln_var, tt + 1)
                        act.activation(mv[0:m, tt, 2:3], mv[0:m, tt, 1:2], ACT.Sqrt, bias=eps[0:m, :]).then_inc(v_std, 1)
                if n == O_AT + 5:
                    act.wait_ge(o_ev, 9)
                    act.activation(osq[:, :, :], qf[:, :, :], ACT.Square).then_inc(o_sq, 1)
                if n == NORM_AT:
                    for h in range(H):
                        act.wait_ge(n_mm, h + 1)
                        act.activation(ostd[:, h, :], psum[4 + h % 4][:, 0:T], ACT.Sqrt, bias=eps, scale=1.0 / P).then_inc(n_std, 1)
                if n == Y_AT:
                    act.wait_ge(upper_free, 1)
                    for br, src in ((0, u), (1, qf)):
                        act.copy(y_parts[:, br, 0, :, :], src).then_inc(yh_ready, 1)
            for r in range(Q_OUT):
                if r + 3 < Q_OUT + 2:
                    hi_part(N_IN + r + 3)
                if r % 2 == 1:
                    act.wait_ge(m_sum, r // 2 + 1)
                    act.copy(m_hi[:, r - 1:r + 1, :], gb[:, r - 1:r + 1, :]).then_inc(mh_ready, 1)
            for j in range(KD):
                hi_part(N_IN + Q_OUT + j + 2)
            act.wait_ge(raw_mm, 1)
            act.copy(lg_fm, psum[7][0:E, 0:T]).then_inc(raw_ev, 1)
            act.wait_ge(l_var, 1)
            act.activation(mv[:, :, 2], mv[:, :, 1], ACT.Sqrt, bias=eps).then_inc(l_std, 1)
            act.wait_ge(l_shift, 1)
            act.activation(x1[0:NS, 2, :], x1[0:NS, 2, :], ACT.Identity, bias=shift[0:NS, :], scale=mv[0:NS, 2, 3:4]).then_inc(x1s_norm, 1)
            act.wait_ge(r_max, 1)
            act.activation(probs, probs, ACT.Exp).then_inc(r_exp, 1)

            def pair(i):
                for a in range(2):
                    act.wait_ge(w_used, i * UNITS + (W_FREE + 12 * a + 8))
                    act.activation(hid[a], psum[2 * a][:, :], ACT.Silu).then_inc(silu, 1)
                    act.wait_ge(hid_tr, i * 2 + (a + 1))
                    act.copy(hidt[a].rearrange("p j f s -> p (j f s)"), psum[6][:, :]).then_inc(hid_ev, 1)

            with act.Fori(0, NPAIR) as i:
                pair(i)
            act.wait_ge(plan_ready, 1)
            pairs = act.value_load(plan[0:1, 0:1], min_val=0, max_val=NOVP)
            with act.If(pairs > 0):
                with act.Fori(0, pairs) as j:
                    pair(j + NPAIR)
            for tt in range(3):
                m = P if tt < 2 else NS
                act.mul(x1[0:m, tt, :], x1[0:m, tt, :], ALPHA).then_inc(ax_ready, 1)
            for w in range(2):
                row = ring_slot(4 + w)[0:NS, 0:D]
                act.wait_ge(r_in[2][w], 16)
                act.activation(row, row, ACT.Identity, scale=cw[0:NS, 2, w:w + 1]).then_inc(s_weighted, 1)
            for n, tt in enumerate((0, 2, 1)):
                m = P if tt < 2 else NS
                act.wait_ge(l_var, n + 2)
                act.activation(mv[0:m, tt, 2:3], mv[0:m, tt, 1:2], ACT.Sqrt, bias=eps[0:m, :]).then_inc(l_std, 1)
                if tt == 2:
                    row = ring_slot(4)[0:NS, 0:D]
                    act.wait_ge(s_shift, 1)
                    act.activation(row, row, ACT.Identity, bias=shift[0:NS, :], scale=mv[0:NS, 2, 3:4]).then_inc(s_norm, 1)

        @block.vector
        def _(dve):
            chain = [0]

            def link(ins):
                chain[0] += 1
                ins.then_inc(dve_chain, 1)
                dve.wait_ge(dve_chain, chain[0])

            def normalise(row, tt, m, lnp, done):
                link(dve.scalar_tensor_tensor(out=row, in0=row, scalar=mv[0:m, tt, 0:1], in1=lnp[0:m, 0, :],
                                              op0=ALU.subtract, op1=ALU.mult))
                dve.scalar_tensor_tensor(out=row, in0=row, scalar=mv[0:m, tt, 3:4], in1=lnp[0:m, 1, :],
                                         op0=ALU.mult, op1=ALU.add).then_inc(done, 1)

            def lo_to(q_end):
                while lo_next[0] <= min(q_end, QUANTA - 1):
                    q = lo_next[0]
                    dve.wait_ge(hi_ready, q + 1)
                    dve.tensor_tensor(w_lo[:, q % 4, :], raw_w[:, q % 4, :], hi_of(q).bitcast(F32), ALU.subtract).then_inc(lo_ready, 1)
                    lo_next[0] += 1

            lo_next = [0]
            dve.memset(up[:, 0:4096], 0.0).then_inc(zeroed, 1)
            lo_to(0)
            for x in range(4):
                dve.wait_ge(xh_ready, x + 1)
                part = slice(4 * x, 4 * x + 4)
                dve.tensor_tensor(x_lo[:, part, :], raw_x[:, part, :], x_hi[:, part, :].bitcast(F32), ALU.subtract).then_inc(xl_ready, 1)
            lo_to(3)
            dve.wait_ge(side_in, 16 * 7)
            dve.wait_ge(consts, 1)
            dve.tensor_tensor(lbw[:, 1, :], lbw[:, 0, :], lbw[:, 0, :], ALU.subtract).then_inc(lb_sub, 1)
            dve.wait_ge(lb_exp, 1)
            link(dve.reciprocal(lbw[:, 2, :], lbw[:, 1, :]))
            link(dve.tensor_tensor(lbw[:, 2, :], lbw[:, 1, :], lbw[:, 2, :], ALU.mult))
            link(dve.tensor_tensor(lbw[:, 3, :], lbw[:, 2, :], lbw[:, 2, :], ALU.subtract))
            link(dve.tensor_scalar(omlb, lbw[:, 3, :], -1.0, 1.0, ALU.mult, ALU.add))
            for h in range(H):
                lo_to(h + 2)
                dve.wait_ge(act_evac, h + 1)
                dve.tensor_scalar(pcum[:, h, :], pcum[:, h, :], omlb[:, h:h + 1], lbw[:, 3, h:h + 1], ALU.mult, ALU.add)
                ins = dve.tensor_scalar(kf[:, h, :], kf[:, h, :], omlb[:, h:h + 1], None, ALU.mult)
            link(ins)
            link(dve.tensor_copy(fqk[:, 0, :, :], pcum[:, :, NP_:T]))
            dve.tensor_copy(fqk[:, 2, :, :], kf[:, :, NP_:T]).then_inc(f_ready, 1)
            lo_to(17)
            dve.wait_ge(act_evac, 16)
            dve.tensor_copy(fqk[:, 1, :, :], qf[:, :, NP_:T]).then_inc(k_ready, 1)

            def evac_tm(tr, ev, dst, batch):
                for tt in range(3):
                    m = P if tt < 2 else NS
                    dve.wait_ge(tr, 3 * batch + tt + 1)
                    dve.tensor_copy(dst[0:m, tt, 512 * batch:512 * batch + 512], psum[4 + tt][0:m, :]).then_inc(ev, 1)

            def copies(lv):
                if lv == 7:
                    for r in range(2):
                        dve.wait_ge(lvl_mm, 4 * 8 + r + 1)
                        dve.tensor_copy(scx[:, 4 * r:4 * r + 4, :], psum[4 + r][:, :].rearrange("p (h t) -> p h t", t=P)).then_inc(lvl_cp, 1)
                    return
                for r in range(4):
                    dve.wait_ge(lvl_mm, 4 * (lv + 1) + r + 1)
                    dve.copy_predicated(sc[:, 2 * r:2 * r + 2, :, :].rearrange("p h a t -> p (h a) t"),
                                        mask[:, lv + 1:lv + 2, :].bitcast(I32).broadcast_to([P, 4, P]),
                                        psum[4 + r][:, :].rearrange("p (h t) -> p h t", t=P)).then_inc(lvl_cp, 1)
                dve.wait_ge(lvl_cp, 4 * (lv + 2))

            def decay(lv, n):
                h = 1 << lv
                dve.wait_ge(lvl_exp, 2 * lv + 2)
                dve.tensor_tensor(halves(z, h, 1), halves(z, h, 1), halves(qf, h, 1), ALU.mult)
                dve.tensor_tensor(halves(z, h, 0), halves(z, h, 0), halves(kf, h, 0), ALU.mult).then_inc(lvl_z, 1)
                lo_to(n + 4)
                link(dve.tensor_tensor(halves(scum, h, 0), halves(scum, h, 0), total(pcum, h, 1), ALU.add))
                dve.tensor_tensor(halves(pcum, h, 1), halves(pcum, h, 1), total(pcum, h, 0), ALU.add).then_inc(lvl_up, 1)
                dve.wait_ge(lvl_up, lv + 1)

            dve.wait_ge(zero_out, 32)
            def level_done(lv, n):
                lo_to(n + 2)
                copies(lv)
                if lv < 7:
                    lo_to(n + 3)
                    decay(lv + 1, n)

            level_done(-1, DIAG_AT)
            level_done(0, LEVEL_AT[0])
            evac_tm(i_tr, i_ev, itm, 0)
            lo_to(I_TR_AT[1] + 2)
            evac_tm(i_tr, i_ev, itm, 1)
            level_done(1, LEVEL_AT[1])
            lo_to(V_TR_AT[0] + 2)
            evac_tm(v_tr, v_ev, vtm, 0)
            level_done(2, LEVEL_AT[2])
            lo_to(V_TR_AT[1] + 2)
            evac_tm(v_tr, v_ev, vtm, 1)
            lo_to(V_TR_AT[1] + 3)
            dve.wait_ge(v_ev, 6)
            for tt in range(3):
                m = P if tt < 2 else NS
                row = vtm[0:m, tt, :]
                for j in range(2):
                    ins = dve.bn_stats(stat[0:m, tt, j, :], row[:, 512 * j:512 * j + 512])
                link(ins)
                dve.bn_aggr(mv[0:m, tt, 0:2], stat[0:m, tt, 0:2, :].rearrange("p n s -> p (n s)")).then_inc(v_ln_var, 1)
                dve.wait_ge(v_ln_var, tt + 1)
            level_done(3, LEVEL_AT[3])
            for tt in range(3):
                lo_to(U0 - 2 + tt)
                m = P if tt < 2 else NS
                row = vtm[0:m, tt, :]
                dve.wait_ge(v_std, tt + 1)
                link(dve.reciprocal(mv[0:m, tt, 3:4], mv[0:m, tt, 2:3]))
                link(dve.tensor_scalar(row, row, mv[0:m, tt, 0:1], mv[0:m, tt, 3:4], ALU.subtract, ALU.mult))
                link(dve.tensor_tensor(row, row, lngb[0:m, 0, :], ALU.mult))
                dve.tensor_tensor(row, row, lngb[0:m, 1, :], ALU.add).then_inc(v_ln, 1)
            for lv in range(4, 8):
                level_done(lv, LEVEL_AT[lv])
            lo_to(KFIN_AT + 1)
            dve.wait_ge(lvl_exp, 17)
            dve.tensor_tensor(z, z, kf[:, :, 0:NP_], ALU.mult).then_inc(kf_ev, 1)
            lo_to(KFIN_AT + 2)
            dve.wait_ge(kf_tr, 4)
            for r in range(4):
                dve.tensor_copy(ktm[:, r // 2, 512 * (r % 2):512 * (r % 2) + 512], psum[4 + r][:, :]).then_inc(kf_ev, 1)
            lo_to(STATE_AT + 2)
            dve.wait_ge(st_mm, 1)
            for r in range(2):
                ins = dve.tensor_copy(scum[:, 4 * r:4 * r + 4, 0:P], psum[4 + r][:, :].rearrange("p (h v) -> p h v", v=P))
            ins.then_inc(st_ev, 1)
            dve.wait_ge(ks_tr, 1)
            for r in range(2):
                ins = dve.tensor_copy(ks_rows[0:NS, 512 * r:512 * r + 512], psum[6 + r][0:NS, :])
            ins.then_inc(ks_ev, 1)
            for h in range(H):
                a = h % 4
                if h >= 2:
                    dve.wait_ge(s_mm, h - 1)
                dve.tensor_tensor(vdb[h % 2], itm[0:NS, 2:3, P * h:P * h + P].broadcast_to([NS, NS, P]),
                                  ident[0:NS, 0:NS].unsqueeze(2).broadcast_to([NS, NS, P]), ALU.mult).then_inc(s_vd, 1)
                dve.wait_ge(s0_in[a], 16 * (h // 4 + 1))
                link(dve.tensor_tensor(s0b[a], s0b[a], fqk[:, 0, h, :].unsqueeze(2).broadcast_to([P, NS, P]), ALU.mult))
                lo_to(SAMPLE_AT + h + 2)
                dve.wait_ge(s_mm, h + 1)
                for r in range(2):
                    ins = dve.tensor_tensor(s0b[a][:, 4 * r:4 * r + 4, :], s0b[a][:, 4 * r:4 * r + 4, :],
                                            psum[4 + r][:, :].rearrange("p (b v) -> p b v", v=P), ALU.add)
                ins.then_inc(s_new, 1)
            for h in range(H):
                lo_to(O_AT + h // 2 + 2)
                dve.wait_ge(o_mm, h + 1)
                dve.tensor_copy(qf[:, h, 0:NP_], psum[(4, 5, 7)[h % 3]][:, 0:NP_]).then_inc(o_ev, 1)
            dve.wait_ge(s_o, 8)
            dve.tensor_copy(qf[:, :, NP_:T], psum[6][:, 0:H * NS].rearrange("p (h b) -> p h b", b=NS)).then_inc(o_ev, 1)
            dve.wait_ge(act_evac, U0 + 8)
            for g in range(H):
                b = psum[(4, 5, 7)[g % 3]][:, 0:NP_].rearrange("p (a t) -> p a t", t=P)
                lo_to(SGU_AT + g // 2 + 2)
                dve.wait_ge(sgu_mm, g + 1)
                link(dve.tensor_tensor(b, b, bsb[:, g:g + 1, :].broadcast_to([P, 2, P]), ALU.add))
                ug = u[:, g, 0:NP_].rearrange("p (a t) -> p a t", t=P)
                dve.tensor_tensor(ug, ug, b, ALU.mult).then_inc(sgu_ev, 1)
            dve.wait_ge(vs_tr, 1)
            vs = psum[6][:, 0:H * NS].rearrange("p (g b) -> p g b", b=NS)
            link(dve.tensor_tensor(vs, vs, w00b.unsqueeze(2).broadcast_to([P, H, NS]), ALU.mult))
            link(dve.tensor_tensor(vs, vs, bsb[:, :, 0:1].broadcast_to([P, H, NS]), ALU.add))
            dve.tensor_tensor(u[:, :, NP_:T], u[:, :, NP_:T], vs, ALU.mult).then_inc(sgu_ev, 1)
            lo_to(NORM_AT + 1)
            dve.wait_ge(o_sq, 1)
            for h in range(H):
                ins = dve.scalar_tensor_tensor(out=qf[:, h, :], in0=qf[:, h, :], scalar=ngain[:, h:h + 1], in1=gf[:, h, :],
                                               op0=ALU.mult, op1=ALU.mult)
            for r in range(4):
                lo_to(NORM_AT + 2 + r)
                two = slice(2 * r, 2 * r + 2)
                dve.wait_ge(n_std, 2 * r + 2)
                ins = dve.reciprocal(ostd[:, two, :], ostd[:, two, :])
            link(ins)
            lo_to(NORM_AT + 6)
            dve.tensor_tensor(qf[:, :, :], qf[:, :, :], ostd[:, :, :], ALU.mult).then_inc(yb_ready, 1)
            dve.wait_ge(yb_ready, 1)
            dve.wait_ge(sgu_ev, 9)
            dve.wait_ge(outs, 16)
            dve.wait_ge(vs_out, 16)
            dve.wait_ge(s_out[2], 32)
            dve.wait_ge(s_out[3], 32)
            dve.nop().then_inc(upper_free, 1)
            for br, src in ((0, u), (1, qf)):
                lo_to(Y_AT + 2 + br)
                dve.wait_ge(yh_ready, br + 1)
                dve.tensor_tensor(y_parts[:, br, 1, :, :], src, y_parts[:, br, 0, :, :].bitcast(F32), ALU.subtract).then_inc(yl_ready, 1)

            def merged_lo(r):
                dve.wait_ge(mh_ready, r + 1)
                two = slice(2 * r, 2 * r + 2)
                dve.tensor_tensor(m_lo[:, two, :], gb[:, two, :], m_hi[:, two, :].bitcast(F32), ALU.subtract).then_inc(ml_ready, 1)

            lo_to(N_IN + 2)
            dve.wait_ge(act_evac, N_IN)
            for r in range(Q_OUT):
                if r == SUMS_AT:
                    dve.wait_ge(router_in, 16 * 4)
                    for a, out in enumerate((rwg, rwb)):
                        ins = dve.tensor_tensor(out, rw_fm, ln1_fm[:, a, :].unsqueeze(2).broadcast_to([P, KD, E]), ALU.mult)
                    ins.then_inc(rw_ready, 1)
                if r == SUMS_AT + 2:
                    dve.wait_ge(sums_mm, 1)
                    for a, out in enumerate((neg_gsum, bsum)):
                        ins = dve.tensor_reduce(out.unsqueeze(2), psum[7][:, KD * E * a:KD * E * (a + 1)].rearrange("p (k e) -> p e k", e=E), AX.X, ALU.add)
                    link(ins)
                    dve.tensor_scalar(neg_gsum, neg_gsum, -1.0, None, ALU.mult)
                    dve.tensor_tensor(bsum, bsum, rbw, ALU.add).then_inc(sums_ready, 1)
                for f in range(2):
                    n = N_IN + 2 * r + f
                    j = 2 * (r // 2) + f
                    dve.wait_ge(gemm, n + 1)
                    if r % 2 == 0:
                        ins = dve.tensor_tensor(ga[:, j, :], ga[:, j, :], psum[n % 4][:, 0:T], ALU.mult)
                        ins.then_inc(dve_evac, 1)
                    else:
                        dve.tensor_tensor(gb[:, j, :], gb[:, j, :], psum[n % 4][:, 0:T], ALU.mult).then_inc(dve_evac, 1)
                if r % 2 == 1:
                    dve.wait_ge(dve_evac, 2 * r + 2)
                    dve.tensor_tensor(gb[:, r - 1:r + 1, :], gb[:, r - 1:r + 1, :], ga[:, r - 1:r + 1, :], ALU.add).then_inc(m_sum, 1)
                lo_to(min(N_IN + r + 3, N_IN + Q_OUT + 1))
                if r % 2 == 0 and r:
                    merged_lo(r // 2 - 1)
            merged_lo(Q_OUT // 2 - 1)

            def h_tm(batch):
                for tt in range(3):
                    m = P if tt < 2 else NS
                    dve.wait_ge(h_tr, 3 * batch + tt + 1)
                    dve.bn_stats(stat[0:m, tt, batch, :], psum[4 + tt][0:m, :])
                    dve.tensor_copy(x1[0:m, tt, 512 * batch:512 * batch + 512], psum[4 + tt][0:m, :]).then_inc(h_ev, 1)

            for j in range(KD):
                n = N_IN + N_OUT + j
                dve.wait_ge(gemm, n + 1)
                if j == 0:
                    link(dve.memset(x1[:, 2, :], 0.0))
                    dve.wait_ge(x_again_in, 16)
                dve.scalar_tensor_tensor(out=xt[:, j, :], in0=xt[:, j, :], scalar=ALPHA, in1=psum[n % 4][:, 0:T],
                                         op0=ALU.mult, op1=ALU.add).then_inc(dve_evac, 1)
                lo_to(N_IN + Q_OUT + j + 2)
                if j % 4 == 1 and j > 4:
                    h_tm(j // 4 - 1)
            link(dve.memset(mv, 1.0))
            h_tm(3)
            dve.wait_ge(h_ev, 12)
            for tt in range(3):
                m = P if tt < 2 else NS
                ins = dve.bn_aggr(mv[0:m, tt, 0:2], stat[0:m, tt, :, :].rearrange("p n s -> p (n s)"))
            ins.then_inc(l_var, 1)
            dve.wait_ge(l_std, 1)
            dve.reciprocal(mv[:, :, 3], mv[:, :, 2]).then_inc(l_inv, 1)
            dve.wait_ge(l_inv, 1)
            dve.scalar_tensor_tensor(out=shift[0:NS, :], in0=mv[0:NS, 2, 0:1], scalar=-1.0, in1=mv[0:NS, 2, 3:4],
                                     op0=ALU.mult, op1=ALU.mult).then_inc(l_shift, 1)

            dve.memset(sel_at, -1.0)
            link(dve.memset(probs, 0.0))
            dve.wait_ge(lg_mm, 1)
            for tt in range(3):
                m = P if tt < 2 else NS
                ins = dve.scalar_tensor_tensor(out=probs[0:m, tt, :], in0=neg_gsum[0:m, :], scalar=mv[0:m, tt, 0:1],
                                               in1=psum[0][0:m, E * tt:E * (tt + 1)], op0=ALU.mult, op1=ALU.add)
            link(ins)
            for tt in range(3):
                m = P if tt < 2 else NS
                ins = dve.scalar_tensor_tensor(out=probs[0:m, tt, :], in0=probs[0:m, tt, :], scalar=mv[0:m, tt, 3:4],
                                               in1=bsum[0:m, :], op0=ALU.mult, op1=ALU.add)
            link(ins)
            link(dve.tensor_reduce(r1[:, :, 0:1], probs, AX.X, ALU.max))
            dve.tensor_tensor(probs, probs, r1[:, :, 0:1].broadcast_to([P, 3, E]), ALU.subtract).then_inc(r_max, 1)
            dve.wait_ge(r_exp, 1)
            link(dve.tensor_reduce(r1[:, :, 0:1], probs, AX.X, ALU.add))
            link(dve.reciprocal(r1[:, :, 0:1], r1[:, :, 0:1]))
            link(dve.tensor_tensor(probs, probs, r1[:, :, 0:1].broadcast_to([P, 3, E]), ALU.mult))

            def flat(a):
                return a.rearrange("p a (g e) -> p (a g) e", e=EG)

            def first_max(src, best, hot, tmp, n):
                link(dve.tensor_reduce(best, src, AX.X, ALU.max))
                link(dve.tensor_tensor(hot, src, best.broadcast_to([P, n, EG]), ALU.is_equal))
                link(dve.tensor_tensor(hot, hot, back4.unsqueeze(1).broadcast_to([P, n, EG]), ALU.mult))
                link(dve.tensor_reduce(tmp, hot, AX.X, ALU.min))
                link(dve.tensor_tensor(hot, tmp.broadcast_to([P, n, EG]), back4.unsqueeze(1).broadcast_to([P, n, EG]), ALU.is_equal))

            first_max(flat(probs), best1, flat(hot1), tmp12, 12)
            link(dve.scalar_tensor_tensor(out=rest, in0=hot1, scalar=-2.0, in1=probs, op0=ALU.mult, op1=ALU.add))
            first_max(flat(rest), best2, flat(hot2), tmp12, 12)
            link(dve.tensor_tensor(gsum, best1, best2, ALU.add))
            g3 = gsum.rearrange("p (a g) o -> p a (g o)", a=3)
            first_max(g3, r1[:, :, 0:1], hotg, r1[:, :, 1:2], 3)
            hg = hotg.rearrange("p a g -> p (a g)").unsqueeze(2)
            for hot, best, w in ((hot1, best1, 0), (hot2, best2, 1)):
                dve.tensor_tensor(flat(hot), flat(hot), hg.broadcast_to([P, 12, EG]), ALU.mult)
                link(dve.tensor_tensor(best, best, hg, ALU.mult))
                link(dve.tensor_reduce(cw[:, :, w:w + 1], best.rearrange("p (a g) o -> p a (g o)", a=3), AX.X, ALU.add))
            link(dve.tensor_reduce(r1[:, :, 0:1], cw, AX.X, ALU.add))
            link(dve.reciprocal(r1[:, :, 0:1], r1[:, :, 0:1]))
            dve.tensor_tensor(cw, cw, r1[:, :, 0:1].broadcast_to([P, 3, 2]), ALU.mult)
            link(dve.tensor_tensor(sel, hot1, hot2, ALU.add))
            dve.tensor_tensor(sel, sel, valid.unsqueeze(2).broadcast_to([P, 3, E]), ALU.mult).then_inc(sel_ready, 1)
            dve.wait_ge(sel_ready, 1)
            dve.wait_ge(ln1_in, 32)
            normalise(x1[:, 0, :], 0, P, ln1p, x1_ready)
            dve.wait_ge(rank_mm, 1)
            link(dve.tensor_copy(rank.rearrange("p a e -> p (a e)"), psum[5][:, 0:3 * E]))
            link(dve.tensor_copy(count, psum[6][:, 0:E]))
            link(dve.tensor_scalar(ranked, rank, FAR, None, ALU.add))
            link(dve.tensor_tensor(ranked, ranked, sel, ALU.mult))
            def choose(p):
                dve.tensor_tensor(pick[:, :, :, :], iota_cap.unsqueeze(1).unsqueeze(1).broadcast_to([P, 3, 2, CAP]),
                                  sel_at[:, :, bass.ds(p * 2, 2)].unsqueeze(3).broadcast_to([P, 3, 2, CAP]), ALU.is_equal).then_inc(picked, 1)

            def take_gathered(p):
                for r in range(4):
                    dve.wait_ge(g_mm, p * 4 + (r + 1))
                    dve.tensor_copy(xg[:, 4 * r:4 * r + 4, :], psum[7 - r % 2][:, :].rearrange("p (k s) -> p k s", s=P)).then_inc(g_ev, 1)

            dve.sem_inc(ob_ready, 1)
            dve.sem_inc(g_ev, 2)
            link(dve.tensor_scalar(sel_at[:, :, 0:E], ranked, -FAR, None, ALU.add))
            choose(0)
            for half in range(2):
                cols = slice(D // 2 * half, D // 2 * (half + 1))
                normalise(x1[:, 1, cols], 1, P, ln1p[:, :, cols], x1_ready)
            take_gathered(0)
            link(dve.tensor_tensor(more, count.unsqueeze(2).broadcast_to([P, E, 4]), b64.unsqueeze(1).broadcast_to([P, E, 4]), ALU.is_gt))
            link(dve.tensor_reduce(nmore, more, AX.X, ALU.add))
            link(dve.tensor_tensor(pair16, ecol.unsqueeze(2).broadcast_to([P, E, E]), ecol.unsqueeze(1).broadcast_to([P, E, E]), ALU.is_gt))
            link(dve.tensor_tensor(pair16, pair16, nmore.unsqueeze(1).broadcast_to([P, E, E]), ALU.mult))
            link(dve.tensor_reduce(cum, pair16, AX.X, ALU.add))
            link(dve.tensor_scalar(bm1, b64, 1.0 / CAP, -1.0, ALU.mult, ALU.add))
            link(dve.tensor_tensor(number, cum.unsqueeze(2).broadcast_to([P, E, 4]), bm1.unsqueeze(1).broadcast_to([P, E, 4]), ALU.add))
            def further_block(j):
                link(dve.tensor_scalar(which, number, float(j), None, ALU.is_equal))
                link(dve.tensor_tensor(which, which, more, ALU.mult))
                for tt in range(3):
                    link(dve.tensor_tensor(wtmp, ranked[:, tt, :].unsqueeze(2).broadcast_to([P, E, 4]), b64.unsqueeze(1).broadcast_to([P, E, 4]), ALU.subtract))
                    link(dve.tensor_tensor(wtmp, wtmp, which, ALU.mult))
                    link(dve.tensor_reduce(r1[:, tt, 0:1], wtmp, AX.XY, ALU.add))
                dve.tensor_scalar(sel_at[:, :, E + j:E + j + 1], r1[:, :, 0:1], -FAR, None, ALU.add)
                link(dve.tensor_tensor(wtmp, which, ecol.unsqueeze(2).broadcast_to([P, E, 4]), ALU.mult))
                link(dve.tensor_reduce(planf[:, 1 + j:2 + j], wtmp, AX.XY, ALU.add))

            def plan_end():
                link(dve.tensor_reduce(planf[:, 0:1], nmore, AX.X, ALU.add))
                link(dve.tensor_scalar(evens, ecol[:, 0:NOVP], 2.0, None, ALU.mult))
                link(dve.tensor_tensor(evens, planf[:, 0:1].broadcast_to([P, NOVP]), evens, ALU.is_gt))
                link(dve.tensor_reduce(planf[:, 0:1], evens, AX.X, ALU.add))
                dve.tensor_copy(plan, planf).then_inc(plan_ready, 1)
                link(dve.tensor_scalar(cum, cum, float(CAP), float(CAP * (E - 1)), ALU.mult, ALU.add))
                link(dve.tensor_tensor(cum, cum, e64, ALU.subtract))
                link(dve.tensor_scalar(rest, rank, float(CAP), None, ALU.is_ge))
                link(dve.tensor_tensor(rest, rest, cum.unsqueeze(1).broadcast_to([P, 3, E]), ALU.mult))
                link(dve.tensor_tensor(rest, rest, rank, ALU.add))
                link(dve.tensor_tensor(rest, rest, e64.unsqueeze(1).broadcast_to([P, 3, E]), ALU.add))
                for w, hot in enumerate((hot1, hot2)):
                    link(dve.tensor_tensor(hot, hot, rest, ALU.mult))
                    link(dve.tensor_reduce(r1[:, :, w:w + 1], hot, AX.X, ALU.add))
                dve.tensor_copy(rowi, r1[:, :, 0:2]).then_inc(rows_ready, 1)

            def hidden(i, a):
                dve.wait_ge(silu, i * 2 + (a + 1))
                dve.tensor_tensor(hid[a], hid[a], psum[2 * a + 1][:, :], ALU.mult).then_inc(hid_ready, 1)

            def result(i, a):
                dve.wait_ge(w_used, i * UNITS + (W_FREE + 12 * a + 12))
                dve.wait_ge(ob_free, i * 2 + (a + 1))
                dve.tensor_copy(ob[a][:, 0, :], psum[4][:, :])
                dve.tensor_copy(ob[a][:, 1, :], psum[5][:, :]).then_inc(ob_ready, 1)

            def pair(i):
                choose(i + 1)
                hidden(i, 0)
                result(i, 0)
                hidden(i, 1)
                take_gathered(i + 1)
                result(i, 1)

            choose(1)
            further_block(0)
            hidden(0, 0)
            for j in range(1, 5):
                further_block(j)
            result(0, 0)
            for j in range(5, NOV):
                further_block(j)
            plan_end()
            hidden(0, 1)
            take_gathered(1)
            result(0, 1)
            with dve.Fori(1, NPAIR) as i:
                pair(i)
            dve.wait_ge(plan_ready, 1)
            pairs = dve.value_load(plan[0:1, 0:1], min_val=0, max_val=NOVP)
            with dve.If(pairs > 0):
                with dve.Fori(0, pairs) as j:
                    pair(j + NPAIR)
            dve.wait_ge(ln2_in, 32)
            dve.wait_ge(ax_ready, 3)
            def mean_and_std(row, tt, m):
                for j in range(4):
                    ins = dve.bn_stats(stat[0:m, tt, j, :], row[:, 512 * j:512 * j + 512])
                link(ins)
                dve.bn_aggr(mv[0:m, tt, 0:2], stat[0:m, tt, :, :].rearrange("p n s -> p (n s)")).then_inc(l_var, 1)
                dve.wait_ge(l_std, (0, 2, 1).index(tt) + 2)
                link(dve.reciprocal(mv[0:m, tt, 3:4], mv[0:m, tt, 2:3]))

            for tt in range(2):
                row, second = ring_slot(2 * tt)[:, 0:D], ring_slot(2 * tt + 1)[:, 0:D]
                dve.wait_ge(r_in[tt][0], 16)
                link(dve.scalar_tensor_tensor(out=row, in0=row, scalar=cw[:, tt, 0:1], in1=x1[:, tt, :], op0=ALU.mult, op1=ALU.add))
                dve.wait_ge(r_in[tt][1], 16)
                link(dve.scalar_tensor_tensor(out=row, in0=second, scalar=cw[:, tt, 1:2], in1=row, op0=ALU.mult, op1=ALU.add))
                mean_and_std(row, tt, P)
                for cols in ((slice(0, D),) if tt == 0 else (slice(0, D // 2), slice(D // 2, D))):
                    normalise(row[:, cols], tt, P, ln2p[:, :, cols], y_ready)
                if tt == 0:
                    dve.wait_ge(s_sum, 1)
                    mean_and_std(ring_slot(4)[0:NS, 0:D], 2, NS)
                    dve.scalar_tensor_tensor(out=shift[0:NS, :], in0=mv[0:NS, 2, 0:1], scalar=-1.0, in1=mv[0:NS, 2, 3:4],
                                             op0=ALU.mult, op1=ALU.mult).then_inc(s_shift, 1)


def kernel(**inputs):
    import numpy as np
    import concourse.bacc as bacc
    from concourse.bass_utils import run_bass_kernel_spmd as run

    a = {k: np.asarray(v) for k, v in inputs.items()}
    f32 = {
        "x_t": np.concatenate([a["x_prompt"][0], a["x_sample"][:, 0]]).T,
        "w_in": a["w_in"][0],
        "ws_t": a["w_s"][0].transpose(2, 0, 1),
        "w00": a["w_s"][0, :, 0, 0],
        "b_s": a["b_s"][0],
        "lng": a["sgu_ln_g"][0], "lnb": a["sgu_ln_b"][0],
        "lbl": a["lb_logits"][0].reshape(H, P).T,
        "normg": a["hgrn_norm_g"][0].reshape(H, P).T,
        "state": a["state_hgrn"][0],
        "woa": a["w_out_a"][0], "wob": a["w_out_b"][0], "wo": a["w_o"][0],
        "ln1g": a["ln1_g"][0], "ln1b": a["ln1_b"][0],
        "rw": a["router_w"], "rb": a["router_b"],
        "wg": a["w_gate"][0], "wu": a["w_up"][0], "wd": a["w_down"][0],
        "ln2g": a["ln2_g"][0], "ln2b": a["ln2_b"][0],
    }
    nc = bacc.Bacc("TRN2", target_bir_lowering=False, num_devices=1)
    arrays, args = {}, []
    for name, v in f32.items():
        arrays[name] = np.ascontiguousarray(v)
        args.append(nc.dram_tensor(name, arrays[name].shape, F32, kind="ExternalInput").ap())
    for name, shape in (("y", (T, D)), ("st_p", (H, P, P)), ("st_s", (NS, H, P, P)), ("v_rows", (NS, W))):
        args.append(nc.dram_tensor(name, shape, F32, kind="ExternalOutput").ap())
    build(nc, *args)
    r = run(nc, [arrays], core_ids=[0]).results[0]
    return (r["y"][:NP_].reshape(1, NP_, D), r["y"][NP_:].reshape(NS, 1, D), r["st_p"].reshape(1, 1, H, P, P),
            r["st_s"].reshape(1, NS, H, P, P), r["v_rows"].reshape(1, NS, 1, W))
```
